# Optimizing a Trainium2 kernel written in Bass

```python
import math
import jax, jax.numpy as jnp
from jax import lax
import numpy as np

D_MODEL = 2048
BATCH = 1
SEQ = 256
DEPTH = 1

N_META = 16
SSM_WIDTH = D_MODEL // 2
SSM_GROUP = 16
SSM_GROUPS = SSM_WIDTH // SSM_GROUP
SSM_STATE = 64
DT_MIN = 1e-3
DT_MAX = 1e-1
HEAD_DIM = 128
N_HEADS = (D_MODEL // 2) // HEAD_DIM
N_KV_HEADS = 2
ATTN_WIDTH = N_HEADS * HEAD_DIM
KV_WIDTH = N_KV_HEADS * HEAD_DIM
WINDOW = 128
BLOCK = 128
N_BRANCH = 2
IN_COLS = SSM_WIDTH + ATTN_WIDTH + 2 * KV_WIDTH + N_BRANCH * D_MODEL
PEER_HEADS = 8
PEER_KEYS = 128
PEER_N_EXPERTS = PEER_KEYS * PEER_KEYS
PEER_QDIM = 256
PEER_TOPK = 16
PEER_TOKEN_BLOCK = 256
NORM_EPS = 1e-6
NEG_INF = -1e30

kernel_name = "hybrid_s5_swa_peer_encoder"

def rms_norm(x, g):
    xf = x.astype(jnp.float32)
    y = xf * lax.rsqrt(jnp.mean(xf * xf, axis=-1, keepdims=True) + NORM_EPS)
    return (y * g.astype(jnp.float32)).astype(x.dtype)

def _s5_discretize(lam_re, lam_im, log_dt, b_re, b_im):
    f32 = jnp.float32
    dt = jnp.exp(log_dt.astype(f32))[:, None]
    lr = lam_re.astype(f32)
    li = lam_im.astype(f32)
    mag = jnp.exp(lr * dt)
    a_re = mag * jnp.cos(li * dt)
    a_im = mag * jnp.sin(li * dt)
    den = lr * lr + li * li
    nr = a_re - 1.0
    ni = a_im
    coef_re = (nr * lr + ni * li) / den
    coef_im = (ni * lr - nr * li) / den
    br = b_re.astype(f32)
    bi = b_im.astype(f32)
    bb_re = coef_re[..., None] * br - coef_im[..., None] * bi
    bb_im = coef_re[..., None] * bi + coef_im[..., None] * br
    return a_re, a_im, bb_re, bb_im

def _complex_linear_combine(e1, e2):
    a1r, a1i, b1r, b1i = e1
    a2r, a2i, b2r, b2i = e2
    ar = a2r * a1r - a2i * a1i
    ai = a2r * a1i + a2i * a1r
    br = a2r * b1r - a2i * b1i + b2r
    bi = a2r * b1i + a2i * b1r + b2i
    return ar, ai, br, bi

def _s5_direction(u_g, a_re, a_im, bb_re, bb_im, c_re, c_im, reverse):
    bu_re = jnp.einsum('lgc,gpc->lgp', u_g, bb_re)
    bu_im = jnp.einsum('lgc,gpc->lgp', u_g, bb_im)
    ar = jnp.broadcast_to(a_re, bu_re.shape)
    ai = jnp.broadcast_to(a_im, bu_re.shape)
    _, _, h_re, h_im = lax.associative_scan(
        _complex_linear_combine, (ar, ai, bu_re, bu_im), reverse=reverse, axis=0)
    cr = c_re.astype(jnp.float32)
    ci = c_im.astype(jnp.float32)
    return jnp.einsum('lgp,gcp->lgc', h_re, cr) - jnp.einsum('lgp,gcp->lgc', h_im, ci)

def s5_mixer(u, lam_re, lam_im, log_dt, b_re, b_im, c_re, c_im, d_skip, w_glu, b_glu):
    f32 = jnp.float32
    L = u.shape[1]
    disc = [_s5_discretize(lam_re[r], lam_im[r], log_dt[r], b_re[r], b_im[r]) for r in range(2)]

    def per_seq(u_seq):
        ug = u_seq.astype(f32).reshape(L, SSM_GROUPS, SSM_GROUP)
        y_fwd = _s5_direction(ug, *disc[0], c_re[0], c_im[0], False)
        y_bwd = _s5_direction(ug, *disc[1], c_re[1], c_im[1], True)
        return (y_fwd + y_bwd).reshape(L, SSM_WIDTH)

    uf = u.astype(f32)
    y = lax.map(per_seq, uf) + d_skip.astype(f32) * uf
    y = jax.nn.gelu(y)
    y = y * jax.nn.sigmoid(y @ w_glu.astype(f32) + b_glu.astype(f32))
    return y.astype(u.dtype)

def _to_layout(t):
    pad = jnp.zeros((t.shape[0], BLOCK - N_META) + t.shape[2:], t.dtype)
    return jnp.concatenate([t[:, :N_META], pad, t[:, N_META:]], axis=1)

def _from_layout(t):
    return jnp.concatenate([t[:, :N_META], t[:, BLOCK:]], axis=1)

def _band(t, nb):
    tb = t.reshape((t.shape[0], nb, BLOCK) + t.shape[2:])
    widths = [(0, 0), (1, 1)] + [(0, 0)] * (tb.ndim - 2)
    tb = jnp.pad(tb, widths)
    return jnp.concatenate([tb[:, :-2], tb[:, 1:-1], tb[:, 2:]], axis=2)

def _alibi_slopes():
    s = 2.0 ** (-8.0 * np.arange(1, N_HEADS + 1) / N_HEADS)
    return jnp.asarray(s, dtype=jnp.float32)

def windowed_gqa(q, k, v, sink):
    f32 = jnp.float32
    bsz = q.shape[0]
    grp = N_HEADS // N_KV_HEADS
    qp = _to_layout(q * (HEAD_DIM ** -0.5))
    kp = _to_layout(k)
    vp = _to_layout(v)
    Lp = qp.shape[1]
    nb = Lp // BLOCK
    idx = jnp.arange(Lp, dtype=jnp.int32)
    is_meta = idx < N_META
    is_real = idx >= BLOCK
    valid = is_meta | is_real
    pos = jnp.where(is_real, idx - BLOCK + N_META, idx)

    qb = qp.reshape(bsz, nb, BLOCK, N_KV_HEADS, grp, HEAD_DIM)
    kb = _band(kp, nb)
    vb = _band(vp, nb)
    pos_q = pos.reshape(nb, BLOCK)
    pos_b = _band(pos[None], nb)[0]
    valid_b = _band(valid[None], nb)[0]
    meta_b = _band(is_meta[None], nb)[0]
    dist = jnp.abs(pos_q[:, :, None] - pos_b[:, None, :]).astype(f32)
    allowed = valid_b[:, None, :] & (~meta_b[:, None, :]) & (dist <= WINDOW)
    slopes = _alibi_slopes().reshape(N_KV_HEADS, grp)
    bias = -slopes[None, :, :, None, None] * dist[:, None, None]

    s_band = jnp.einsum('bnqkgd,bnskd->bnkgqs', qb, kb, preferred_element_type=f32)
    s_band = jnp.where(allowed[:, None, None], s_band + bias, NEG_INF)
    k_meta = k[:, :N_META]
    v_meta = v[:, :N_META]
    s_meta = jnp.einsum('bnqkgd,bmkd->bnkgqm', qb, k_meta, preferred_element_type=f32)
    sink_l = jnp.broadcast_to(sink.astype(f32).reshape(N_KV_HEADS, grp)[None, None, :, :, None, None],
                              s_meta.shape[:-1] + (1,))
    p = jax.nn.softmax(jnp.concatenate([s_band, s_meta, sink_l], axis=-1), axis=-1)
    p_band = p[..., :3 * BLOCK].astype(v.dtype)
    p_meta = p[..., 3 * BLOCK:3 * BLOCK + N_META].astype(v.dtype)
    out = (jnp.einsum('bnkgqs,bnskd->bnqkgd', p_band, vb)
           + jnp.einsum('bnkgqm,bmkd->bnqkgd', p_meta, v_meta))
    out = out.reshape(bsz, Lp, ATTN_WIDTH)
    return _from_layout(out)

def peer_ffn(h, w_q, sub_k1, sub_k2, u_emb, v_emb):
    f32 = jnp.float32
    bsz, L, D = h.shape
    ht = h.reshape(-1, D)
    T = ht.shape[0]
    half = PEER_QDIM // 2
    q = (ht @ w_q).reshape(T, PEER_HEADS, 2, half)
    s1 = jnp.einsum('thd,hnd->thn', q[:, :, 0], sub_k1, preferred_element_type=f32)
    s2 = jnp.einsum('thd,hnd->thn', q[:, :, 1], sub_k2, preferred_element_type=f32)
    v1, i1 = lax.top_k(s1, PEER_TOPK)
    v2, i2 = lax.top_k(s2, PEER_TOPK)
    cand = (v1[..., :, None] + v2[..., None, :]).reshape(T, PEER_HEADS, PEER_TOPK * PEER_TOPK)
    sc, ci = lax.top_k(cand, PEER_TOPK)
    e1 = jnp.take_along_axis(i1, ci // PEER_TOPK, axis=-1)
    e2 = jnp.take_along_axis(i2, ci % PEER_TOPK, axis=-1)
    eidx = e1 * PEER_KEYS + e2
    gate = jax.nn.softmax(sc, axis=-1)

    pad = (-T) % PEER_TOKEN_BLOCK
    nc = (T + pad) // PEER_TOKEN_BLOCK
    ht_p = jnp.pad(ht, ((0, pad), (0, 0))).reshape(nc, PEER_TOKEN_BLOCK, D)
    e_p = jnp.pad(eidx, ((0, pad), (0, 0), (0, 0))).reshape(nc, PEER_TOKEN_BLOCK, PEER_HEADS, PEER_TOPK)
    g_p = jnp.pad(gate, ((0, pad), (0, 0), (0, 0))).reshape(nc, PEER_TOKEN_BLOCK, PEER_HEADS, PEER_TOPK)

    def block(args):
        hc, ec, gc = args
        u = jnp.take(u_emb, ec, axis=0)
        a = jnp.einsum('cd,chkd->chk', hc, u, preferred_element_type=f32)
        w = (gc * jax.nn.gelu(a)).astype(hc.dtype)
        vv = jnp.take(v_emb, ec, axis=0)
        return jnp.einsum('chk,chkd->cd', w, vv).astype(hc.dtype)

    out = lax.map(block, (ht_p, e_p, g_p))
    return out.reshape(-1, D)[:T].reshape(bsz, L, D)

def setup_inputs(seed: int = 0) -> dict:
    key = jax.random.key(seed)
    ks = jax.random.split(key, 28)
    f32 = jnp.float32

    def nrm(k, shape, scale):
        return jax.random.normal(k, shape, f32) * scale

    G, P, C = SSM_GROUPS, SSM_STATE, SSM_GROUP
    n = jnp.arange(P, dtype=f32)
    return {
        "x": nrm(ks[0], (BATCH, SEQ, D_MODEL), 1.0),
        "meta_tokens": nrm(ks[1], (N_META, D_MODEL), 1.0),
        "norm_mix": 1.0 + nrm(ks[2], (DEPTH, D_MODEL), 0.05),
        "w_in": nrm(ks[3], (DEPTH, D_MODEL, IN_COLS), D_MODEL ** -0.5),
        "b_gate": nrm(ks[4], (DEPTH, N_BRANCH * D_MODEL), 0.02),
        "ssm_lam_re": -0.5 + nrm(ks[5], (DEPTH, 2, G, P), 0.01),
        "ssm_lam_im": math.pi * n + nrm(ks[6], (DEPTH, 2, G, P), 0.01),
        "ssm_log_dt": jax.random.uniform(ks[7], (DEPTH, 2, G), f32, math.log(DT_MIN), math.log(DT_MAX)),
        "ssm_b_re": nrm(ks[8], (DEPTH, 2, G, P, C), (2.0 * C) ** -0.5),
        "ssm_b_im": nrm(ks[9], (DEPTH, 2, G, P, C), (2.0 * C) ** -0.5),
        "ssm_c_re": nrm(ks[10], (DEPTH, 2, G, C, P), 0.5),
        "ssm_c_im": nrm(ks[11], (DEPTH, 2, G, C, P), 0.5),
        "ssm_d": nrm(ks[12], (DEPTH, SSM_WIDTH), 1.0),
        "ssm_w_glu": nrm(ks[13], (DEPTH, SSM_WIDTH, SSM_WIDTH), SSM_WIDTH ** -0.5),
        "ssm_b_glu": nrm(ks[14], (DEPTH, SSM_WIDTH), 0.02),
        "attn_sink": nrm(ks[15], (DEPTH, N_HEADS), 1.0),
        "w_proj_ssm": nrm(ks[16], (DEPTH, SSM_WIDTH, D_MODEL), SSM_WIDTH ** -0.5),
        "w_proj_attn": nrm(ks[17], (DEPTH, ATTN_WIDTH, D_MODEL), ATTN_WIDTH ** -0.5),
        "w_out": nrm(ks[18], (DEPTH, D_MODEL, D_MODEL), D_MODEL ** -0.5),
        "norm_ffn": 1.0 + nrm(ks[19], (DEPTH, D_MODEL), 0.05),
        "peer_w_q": nrm(ks[20], (DEPTH, D_MODEL, PEER_HEADS * PEER_QDIM), D_MODEL ** -0.5),
        "peer_k1": nrm(ks[21], (DEPTH, PEER_HEADS, PEER_KEYS, PEER_QDIM // 2), (PEER_QDIM // 2) ** -0.5),
        "peer_k2": nrm(ks[22], (DEPTH, PEER_HEADS, PEER_KEYS, PEER_QDIM // 2), (PEER_QDIM // 2) ** -0.5),
        "peer_u": nrm(ks[23], (DEPTH, PEER_N_EXPERTS, D_MODEL), D_MODEL ** -0.5),
        "peer_v": nrm(ks[24], (DEPTH, PEER_N_EXPERTS, D_MODEL), 0.5),
        "norm_final": 1.0 + nrm(ks[25], (D_MODEL,), 0.05),
    }

def reference(x, meta_tokens, norm_mix, w_in, b_gate, ssm_lam_re, ssm_lam_im, ssm_log_dt,
              ssm_b_re, ssm_b_im, ssm_c_re, ssm_c_im, ssm_d, ssm_w_glu, ssm_b_glu, attn_sink,
              w_proj_ssm, w_proj_attn, w_out, norm_ffn, peer_w_q, peer_k1, peer_k2, peer_u,
              peer_v, norm_final):
    bsz = x.shape[0]
    meta = jnp.broadcast_to(meta_tokens.astype(x.dtype)[None], (bsz, N_META, D_MODEL))
    hs = jnp.concatenate([meta, x], axis=1)
    L = hs.shape[1]
    splits = [SSM_WIDTH, SSM_WIDTH + ATTN_WIDTH, SSM_WIDTH + ATTN_WIDTH + KV_WIDTH,
              SSM_WIDTH + ATTN_WIDTH + 2 * KV_WIDTH]
    for l in range(DEPTH):
        h = rms_norm(hs, norm_mix[l])
        z = h @ w_in[l]
        u_ssm, q, k, v, gates = jnp.split(z, splits, axis=-1)
        y_a = s5_mixer(u_ssm, ssm_lam_re[l], ssm_lam_im[l], ssm_log_dt[l], ssm_b_re[l], ssm_b_im[l],
                       ssm_c_re[l], ssm_c_im[l], ssm_d[l], ssm_w_glu[l], ssm_b_glu[l])
        y_b = windowed_gqa(q.reshape(bsz, L, N_HEADS, HEAD_DIM),
                           k.reshape(bsz, L, N_KV_HEADS, HEAD_DIM),
                           v.reshape(bsz, L, N_KV_HEADS, HEAD_DIM), attn_sink[l])
        g = jax.nn.sigmoid((gates + b_gate[l]).astype(jnp.float32)).astype(hs.dtype)
        g = g.reshape(bsz, L, N_BRANCH, D_MODEL)
        merged = g[:, :, 0] * (y_a @ w_proj_ssm[l]) + g[:, :, 1] * (y_b @ w_proj_attn[l])
        hs = hs + merged @ w_out[l]
        hs = hs + peer_ffn(rms_norm(hs, norm_ffn[l]), peer_w_q[l], peer_k1[l], peer_k2[l],
                           peer_u[l], peer_v[l])
    hs = rms_norm(hs, norm_final)
    return hs[:, N_META:]


_drawn_inputs = setup_inputs


def setup_inputs(seed=0):
    import zlib

    import numpy as np

    out = dict(_drawn_inputs(seed))
    spreads = {}
    factors = {'b_gate': 5.237, 'ssm_lam_re': 6.799, 'ssm_b_glu': 5.101, 'attn_sink': 5.299}
    for name, (base, spread) in spreads.items():
        noise = np.random.default_rng([zlib.crc32(name.encode()), seed]).standard_normal(out[name].shape)
        drawn = base * np.exp(spread * noise) if base else spread * noise
        out[name] = __import__('jax').numpy.asarray(drawn.astype(out[name].dtype))
    for name, factor in factors.items():
        out[name] = (out[name] * factor).astype(out[name].dtype)
    return out
```

```python
from contextlib import ExitStack

import concourse.bass as bass
from concourse import mybir
import numpy as np

F32 = mybir.dt.float32
U32 = mybir.dt.uint32
ALU = mybir.AluOpType
ACT = mybir.ActivationFunctionType
AX_X = mybir.AxisListType.X

P = 128
D = 2048
KT = D // P
META, SEQ = 16, 256
L = META + SEQ
TT = SEQ // P
SSM_W, GROUPS, GC, ST = 1024, 64, 16, 64
CT = SSM_W // P
NST = 2 * GROUPS * ST // P
SPC = NST // CT
HEADS, KVH, HD = 8, 2, 128
WINDOW = 128
GATES = 2 * D // P
PH, NK, TOPK = 8, 128, 16
EPS = 1e-6
RING = 4
NEG = -3.0e38
MAGIC = 1.5 * 2.0 ** 23
TWO_PI = 6.283185
HALF_PI = float(np.pi / 2)
UV = 4

W_UK, W_V, W_Q, W_GATE, W_GLU, W_PROJ, W_OUT, W_PQ, W_END = 0, 10, 12, 20, 52, 56, 72, 88, 104

COLS, _at = {}, 0
for _name, _n in (("gmix", KT), ("bgate", GATES), ("dskip", CT), ("bglu", CT), ("sink", HEADS),
                  ("lam_re", NST), ("lam_im", NST), ("log_dt", NST), ("iota", L), ("ident", P),
                  ("alibi", TT * L), ("iota16", TOPK)):
    COLS[_name] = (_at, _at + _n)
    _at += _n
NPAR = _at
NSC = 6


def build(nc, W, keys, par, bw, cw, meta, x, gffn, gfin, u_tab, v_tab, out):
    top = ExitStack()
    with top:
        def sem(name):
            return top.enter_context(nc.semaphore(name))

        def sbt(stack, name, shape, dt=F32):
            return stack.enter_context(nc.sbuf_tensor(name, shape, dt))

        prm = sbt(top, "prm", [P, NPAR])
        ring = sbt(top, "ring", [P, RING, D])
        xn = sbt(top, "xn", [P, TT, D])
        hs2 = sbt(top, "hs2", [P, TT, D])
        zeros = sbt(top, "zeros", [1, 640])
        st = sbt(top, "st", [P, 16])
        halfpi = sbt(top, "halfpi", [P, 1])

        mix = ExitStack()
        hT = sbt(mix, "hT", [P, KT * L])
        ukT = sbt(mix, "ukT", [P, 10, L])
        vm = sbt(mix, "vm", [META, KVH * HD])
        vr = sbt(mix, "vr", [P, TT, KVH * HD])
        ybT = sbt(mix, "ybT", [P, HEADS, SEQ])
        yT = sbt(mix, "yT", [P, CT, SEQ])
        gates = sbt(mix, "gates", [P, GATES * SEQ])
        qT = sbt(mix, "qT", [P, 2, SEQ])
        pr = sbt(mix, "pr", [P, 2, L + 1])
        pT = sbt(mix, "pT", [P, 2, 3 * P])
        sm = sbt(mix, "sm", [P, 2, 4])
        scal = sbt(mix, "scal", [P, CT, NSC, SPC])
        scur = sbt(mix, "scur", [P, 2, NSC, SPC])
        ucur = sbt(mix, "ucur", [P, 2, L])
        bwt = sbt(mix, "bwt", [P, 2, 2, 2, P])
        cwt = sbt(mix, "cwt", [P, 2, SPC, 2, 32])
        cp = sbt(mix, "cp", [P, 2, 3, SPC, 32])
        cs = sbt(mix, "cs", [P, 4, SPC, 32])
        tb = sbt(mix, "tb", [P, 2, L])
        ang = sbt(mix, "ang", [P, 2, 2, L])
        trig = sbt(mix, "trig", [P, 4, 2, L])
        pa = sbt(mix, "pa", [P, 2, 2, L])
        pb = sbt(mix, "pb", [P, 2, 2, L])
        gin = sbt(mix, "gin", [P, 2, 2, L])
        mix.close()
        h2f = hs2[:, :, :].rearrange("p t d -> p (t d)")

        def in_hs2(at):
            return h2f[:, at * 4 * L:(at + 1) * 4 * L].rearrange("p (s r t) -> p s r t", s=2, r=2)
        gst, oc, os_ = in_hs2(0), in_hs2(1), in_hs2(2)
        lg = h2f[:, 12 * L:12 * L + 2 * (L + 1)].rearrange("p (s t) -> p s t", s=2)
        disc = gates[:, 3 * D:3 * D + 24 * NST].rearrange("p (k n) -> p k n", k=24)
        xs = gates[:, 0:3 * D].rearrange("p (t d) -> p t d", t=3)
        hTv = hT[:, :].rearrange("p (k t) -> p k t", k=KT)
        mT = hT[:, 0:KT * SEQ].rearrange("p (k t) -> p k t", k=KT)
        yaT = ukT[:, :, :].rearrange("p a t -> p (a t)")[:, 0:CT * SEQ].rearrange("p (k t) -> p k t", k=CT)
        gt = gates[:, :].rearrange("p (b k t) -> p b k t", b=2, k=KT)

        exp_ = ExitStack()
        uv = sbt(exp_, "uv", [P, UV, 2, D])
        h2T = sbt(exp_, "h2T", [P, KT, SEQ])
        sct = sbt(exp_, "sct", [P, TT, PH, 2 * NK])
        keyt = sbt(exp_, "keyt", [P, PH, 2, NK])
        gb = sbt(exp_, "gb", [P, 2, D])
        qp = sbt(exp_, "qp", [P, 2, SEQ])
        dg = sbt(exp_, "dg", [P, 2, P])
        ks = sbt(exp_, "ks", [P, 2 * NK])
        kr = sbt(exp_, "kr", [P, 2 * NK])
        tv = sbt(exp_, "tv", [P, 3, TOPK])
        ti = sbt(exp_, "ti", [P, 3, TOPK], U32)
        tif = sbt(exp_, "tif", [P, 4, TOPK])
        tq = sbt(exp_, "tq", [P, 2, TOPK], U32)
        cand = sbt(exp_, "cand", [P, TOPK, TOPK])
        oh = sbt(exp_, "oh", [P, TOPK, TOPK])
        eid = sbt(exp_, "eid", [P, 2, TOPK], U32)
        gw = sbt(exp_, "gw", [P, 2, TOPK])
        gsum = sbt(exp_, "gsum", [P, 4])
        av = sbt(exp_, "av", [P, 2, TOPK])
        ga = sbt(exp_, "ga", [P, 2, TOPK])
        exp_.close()

        ps = top.enter_context(nc.psum_tensor("ps", [P, 8, 512], F32))

        def col(name, a=0, b=None):
            lo, hi = COLS[name]
            return prm[:, lo + a:hi if b is None else lo + b]

        ident = col("ident")
        iota = col("iota")
        alibi = col("alibi").rearrange("p (b t) -> p b t", b=TT)

        def wtile(n, m, c):
            return ring[:, n % RING, :].rearrange("p (m c) -> p m c", m=m, c=c)

        s_par, s_zero = sem("s_par"), sem("s_zero")
        s_x = [sem(f"s_x{t}") for t in range(TT + 1)]
        s_w = [sem(f"s_w{i}") for i in range(RING)]
        s_wdone = sem("s_wdone")
        s_v = sem("s_v")
        s_tr = sem("s_tr")
        s_trig0, s_f0 = sem("s_trig0"), sem("s_f0")
        s_sq, s_ms, s_sqr, s_xs = sem("s_sq"), sem("s_ms"), sem("s_sqr"), sem("s_xs")
        s_hT = sem("s_hT")
        s_uk = sem("s_uk")
        s_vp, s_ve = sem("s_vp"), sem("s_ve")
        s_qT = [sem("s_qT0"), sem("s_qT1")]
        s_sc, s_lg, s_nm, s_pe, s_pn, s_pt, s_pT, s_av, s_yb = (
            sem(n) for n in ("s_sc", "s_lg", "s_nm", "s_pe", "s_pn", "s_pt", "s_pT", "s_av", "s_yb"))
        s_al = sem("s_al")
        s_bw = [sem("s_bw0"), sem("s_bw1")]
        s_cw = [sem("s_cw0"), sem("s_cw1")]
        s_scur, s_cpl = sem("s_scur"), sem("s_cpl")
        s_cp = sem("s_cp")
        s_bu = sem("s_bu")
        s_vl = sem("s_vl")
        s_ang, s_trg = sem("s_ang"), sem("s_trg")
        s_ab = sem("s_ab")
        s_gin = sem("s_gin")
        s_gst = sem("s_gst")
        s_oc, s_os = sem("s_oc"), sem("s_os")
        s_y = sem("s_y")
        s_ye = sem("s_ye")
        s_gs = sem("s_gs")
        s_gel, s_sgg, s_glu, s_sig, s_ya = sem("s_gel"), sem("s_sgg"), sem("s_glu"), sem("s_sig"), sem("s_ya")
        s_pm, s_mT = sem("s_pm"), sem("s_mT")
        s_hs = sem("s_hs")
        s_kd, s_gbd = sem("s_kd"), sem("s_gbd")
        s_sq2, s_ms2, s_rt2, s_h2, s_t2, s_h2T = (
            sem(n) for n in ("s_sq2", "s_ms2", "s_rt2", "s_h2", "s_t2", "s_h2T"))
        s_qp = sem("s_qp")
        s_ps, s_psc = sem("s_ps"), sem("s_psc")
        s_tk, s_gm, s_gex, s_eid = sem("s_tk"), sem("s_gm"), sem("s_gex"), sem("s_eid")
        s_u = [sem(f"s_u{i}") for i in range(UV)]
        s_vv = [sem(f"s_vv{i}") for i in range(UV)]
        s_dot = sem("s_dot")
        s_gl = sem("s_gl")
        s_dg = sem("s_dg")
        s_ex = sem("s_ex")
        s_lone, s_lonev = sem("s_lone"), sem("s_lonev")
        s_acc, s_fh, s_fsq, s_frt, s_fin, s_out = (
            sem(n) for n in ("s_acc", "s_fh", "s_fsq", "s_frt", "s_fin", "s_out"))

        RPL = 2 * SPC
        gates_v = gates[:, :].rearrange("p (g t) -> p g t", g=GATES)
        block = top.enter_context(nc.Block())

        def flat(ap):
            return ap.rearrange("p a n -> p (a n)")

        @block.sync
        def _(sp):
            def load_weights(n0, i):
                for s in range(RING):
                    sp.wait_ge(s_wdone, n0 + s + 1 + RING * i)
                    sp.dma_start(ring[:, (n0 + s) % RING, :],
                                 W[bass.ds(n0 + s + RING * i, 1), :, :].rearrange("a p n -> (a p) n")
                                 ).then_inc(s_w[(n0 + s) % RING], 16)

            sp.dma_start(prm[:, :], par).then_inc(s_par, 16)
            for t in range(TT):
                sp.dma_start(xn[:, t, :], x[t * P:(t + 1) * P, :]).then_inc(s_x[t], 16)
            sp.dma_start(xs[0:META, TT, :], meta).then_inc(s_x[TT], 16)
            with sp.Fori(0, W_GATE // RING) as i:
                load_weights(0, i)
            with sp.Fori(0, CT // 2) as b:
                for cc in range(2):
                    sp.wait_ge(s_bu, SPC * (2 * b + cc) + 8)
                    sp.dma_start(bwt[:, cc, :, :, :].rearrange("p d r s -> p (d r s)"),
                                 bw[bass.ds(2 * b + cc, 1), :, :].rearrange("a p n -> (a p) n")).then_inc(s_bw[cc], 16)
                    sp.wait_ge(s_cp, 3 * (2 * b + cc) + 3)
                    sp.dma_start(cwt[:, cc, :, :, :].rearrange("p i r c -> p (i r c)"),
                                 cw[bass.ds(2 * b + cc, 1), :, :].rearrange("a p n -> (a p) n")).then_inc(s_cw[cc], 16)
                    load_weights(W_GATE + 4 * cc, 2 * b)
            with sp.Fori(0, (W_PQ - W_GLU) // RING) as i:
                load_weights(W_GLU, i)
            sp.wait_ge(s_hs, 4 + TT * 4)
            sp.dma_start(gb[:, 0, :], gffn).then_inc(s_gbd, 16)
            load_weights(W_PQ, 0)
            sp.dma_start(keyt[:, :, :, :].rearrange("p h s n -> p (h s n)"), keys).then_inc(s_kd, 16)
            sp.dma_start(gb[:, 1, :], gfin).then_inc(s_kd, 16)
            with sp.Fori(0, (W_END - W_PQ) // RING - 1) as i:
                load_weights(W_PQ + RING, i)
            for t in range(TT):
                sp.wait_ge(s_fin, t + 1)
                sp.dma_start(out[t * P:(t + 1) * P, :], xn[:, t, :]).then_inc(s_out, 16)
            sp.wait_ge(s_out, 16 * TT)

        @block.gpsimd
        def _(pool):
            pool.sem_inc(s_cp, 6)
            pool.sem_inc(s_os, 4)
            with pool.Fori(0, CT // 2) as b:
                def out_matrices(cc):
                    ct = 2 * b + cc
                    pool.wait_ge(s_scur, 2 * ct + 2)
                    pool.wait_ge(s_cw[cc], 16 * b + 16)
                    cre, cim = cwt[:, cc, :, 0, :], cwt[:, cc, :, 1, :]

                    def co(k):
                        return scur[:, cc, k, :].rearrange("p (i o) -> p i o", o=1).broadcast_to([P, SPC, 32])
                    if cc == 0:
                        pool.wait_ge(s_cp, 6 * b + 6)
                    else:
                        pool.wait_ge(s_cp, 6 * b + 9)
                    pool.tensor_tensor(cs[:, 0], cre, co(2), ALU.mult).then_inc(s_cpl, 1)
                    pool.tensor_tensor(cs[:, 1], cim, co(3), ALU.mult).then_inc(s_cpl, 1)
                    pool.tensor_tensor(cs[:, 2], cre, co(4), ALU.mult).then_inc(s_cpl, 1)
                    pool.tensor_tensor(cs[:, 3], cim, co(2), ALU.mult).then_inc(s_cpl, 1)
                    pool.wait_ge(s_cpl, 4 * ct + 4)
                    pool.wait_ge(s_y, SPC * ct + 8)
                    pool.tensor_tensor(cp[:, cc, 0], cs[:, 0], cs[:, 1], ALU.subtract).then_inc(s_cp, 1)
                    pool.tensor_tensor(cp[:, cc, 1], cs[:, 1], cs[:, 0], ALU.subtract).then_inc(s_cp, 1)
                    pool.tensor_tensor(cp[:, cc, 2], cs[:, 2], cs[:, 3], ALU.subtract).then_inc(s_cp, 1)

                def turn_inputs(t):
                    s, n = t % 2, RPL * b + t
                    pool.wait_ge(s_ab, 2 * n + 6)
                    pool.wait_ge(s_gst, 2 * n + 2)
                    pool.tensor_tensor(gin[:, s, 0], pa[:, s, 0], pb[:, s, 0], ALU.add).then_inc(s_gin, 1)
                    pool.tensor_tensor(gin[:, s, 1], pa[:, s, 1], pb[:, s, 1], ALU.subtract).then_inc(s_gin, 1)

                def sin_products(t):
                    s, n = t % 2, RPL * b + t
                    pool.wait_ge(s_gst, 2 * n + 6)
                    pool.wait_ge(s_y, n + 15)
                    pool.tensor_tensor(os_[:, s], trig[:, t % 4, 1:2, :].broadcast_to([P, 2, L]), gst[:, s],
                                       ALU.mult).then_inc(s_os, 1)

                for t in range(RPL):
                    if t % SPC == 0:
                        out_matrices(t // SPC)
                    turn_inputs(t)
                    if t >= 1:
                        sin_products(t - 1)
                sin_products(RPL - 1)
            for T in range(TT):
                with pool.Fori(0, PH // 2) as g:
                    for hh in range(2):
                        hd = T * PH + 2 * g + hh
                        pool.wait_ge(s_eid, hd + 1)
                        for j in range(TOPK):
                            m = hd * TOPK + j
                            s = j % UV
                            at = bass.IndirectOffsetOnAxis(ap=eid[:, hh, j:j + 1], axis=0)
                            pool.wait_ge(s_dot, m + 1)
                            pool.sem_inc(s_lone, 1)
                            pool.indirect_dma_start(uv[:, s, 0, :], None, u_tab, at).then_inc(s_u[s], 16)
                            pool.wait_ge(s_ex, m + 1)
                            pool.sem_inc(s_lone, 1)
                            pool.indirect_dma_start(uv[:, s, 1, :], None, v_tab, at).then_inc(s_vv[s], 16)

        @block.scalar
        def _(act):
            act.sem_inc(s_hT, 2)
            act.sem_inc(s_uk, 2)
            act.sem_inc(s_qT[0], 1)
            act.sem_inc(s_qT[1], 1)
            act.sem_inc(s_gs, 2)
            act.sem_inc(s_h2T, 2)
            act.sem_inc(s_qp, 2)
            act.sem_inc(s_psc, 2)
            act.wait_ge(s_f0, 1)
            nc.scalar.activation(disc[:, 6, :], disc[:, 4, :], ACT.Sin, scale=TWO_PI).then_inc(s_trig0, 1)
            nc.scalar.activation(disc[:, 7, :], disc[:, 4, :], ACT.Sin, scale=TWO_PI / 2).then_inc(s_trig0, 1)
            for t in range(TT + 1):
                rows = P if t < TT else META
                src = xn[:, t, :] if t < TT else xs[0:META, TT, :]
                act.wait_ge(s_x[t], 16)
                if t == 0:
                    act.wait_ge(s_ms, 1)
                if t > 0:
                    act.wait_ge(s_sq, t)
                nc.scalar.activation(hT[0:rows, 0:D], src, ACT.Square, accum_out=st[0:rows, t:t + 1]).then_inc(s_sq, 1)
            act.wait_ge(s_ms, 2)
            nc.scalar.activation(st[:, 4:7], st[:, 3 + 4:3 + 7], ACT.Sqrt).then_inc(s_sqr, 1)
            for k in range(KT):
                act.wait_ge(s_tr, k + 1)
                nc.scalar.activation(hTv[:, k, :], ps[:, k % 2, 0:L], ACT.Copy, scale=col("gmix", k, k + 1)).then_inc(s_hT, 1)
            for m in range(W_V):
                act.wait_ge(s_wdone, RING + m + 1)
                nc.scalar.activation(ukT[:, m, :], ps[:, m % 2, 0:L], ACT.Copy).then_inc(s_uk, 1)
            for t in range(TT):
                act.wait_ge(s_vp, t + 1)
                nc.scalar.activation(vr[:, t, :], ps[:, 2 + t, 0:KVH * HD], ACT.Copy).then_inc(s_ve, 1)
            act.wait_ge(s_wdone, RING + W_Q)
            nc.scalar.activation(vm[:, :], ps[0:META, 4, 0:KVH * HD], ACT.Copy).then_inc(s_ve, 1)

            def queries(h):
                act.wait_ge(s_wdone, RING + W_Q + h + 1)
                if h >= 2:
                    act.wait_ge(s_sc, 2 * (h - 1))
                nc.scalar.activation(qT[:, h % 2, :], ps[:, h % 2, 0:SEQ], ACT.Copy, scale=HD ** -0.5
                                     ).then_inc(s_qT[h % 2], 1)

            queries(0)
            for h in range(HEADS):
                for qb in range(TT):
                    a = 2 * h + qb
                    act.wait_ge(s_nm, a + 1)
                    if a >= 2:
                        act.wait_ge(s_pt, a - 1)
                    nc.scalar.activation(pr[:, qb, :], lg[:, qb, :], ACT.Exp, bias=sm[:, qb, 0:1],
                                         accum_out=sm[:, qb, 1:2]).then_inc(s_pe, 1)
                    if qb == 1 and h + 1 < HEADS:
                        queries(h + 1)

            with act.Fori(0, CT // 2) as b:
                def gate(q):
                    g = SPC * b + q
                    act.wait_ge(s_wdone, RING + W_GATE + 1 + g)
                    nc.scalar.activation(flat(gates_v[:, bass.ds(g, 1), :]), ps[:, q % 2, 0:SEQ], ACT.Identity,
                                         bias=prm[:, bass.ds(COLS["bgate"][0] + g, 1)]).then_inc(s_gs, 1)

                for t in range(RPL):
                    n = RPL * b + t
                    act.wait_ge(s_ang, n + 1)
                    act.wait_ge(s_oc, n + 1)
                    act.wait_ge(s_os, n + 1)
                    nc.scalar.activation(trig[:, t % 4, 1, :], ang[:, t % 2, 0, :], ACT.Sin, scale=-TWO_PI
                                         ).then_inc(s_trg, 1)
                    nc.scalar.activation(trig[:, t % 4, 0, :], ang[:, t % 2, 1, :], ACT.Sin, scale=-TWO_PI,
                                         bias=halfpi[:, :]).then_inc(s_trg, 1)
                    if t >= 3 and t % 2:
                        gate((t - 3) // 2)
                gate(SPC - 1)
            act.wait_ge(s_ye, 2 + CT)
            nc.scalar.activation(yT[:, :, :], yT[:, :, :], ACT.Gelu_apprx_tanh).then_inc(s_gel, 1)
            act.wait_ge(s_gs, 2 + GATES)
            nc.scalar.activation(gates[:, :], gates[:, :], ACT.Sigmoid).then_inc(s_sgg, 1)
            for m in range(CT):
                if m % 2 == 0:
                    act.wait_ge(s_glu, m // 2 + 1)
                else:
                    act.wait_ge(s_wdone, RING + W_GLU + m // 2 + 1)
                if m >= 2:
                    act.wait_ge(s_ya, m - 1)
                nc.scalar.activation(qT[:, m % 2, :], ps[:, m % 2, 0:SEQ], ACT.Sigmoid, bias=col("bglu", m, m + 1)
                                     ).then_inc(s_sig, 1)
            for T in range(TT):
                act.wait_ge(s_hs, 4 + TT * 4)
                act.wait_ge(s_ms2, 1)
                nc.scalar.activation(uv[:, 0, 0, :] if T == 0 else uv[:, 0, 1, :], hs2[:, T, :], ACT.Square,
                                     accum_out=st[:, T:T + 1]).then_inc(s_sq2, 1)
            act.wait_ge(s_ms2, 2)
            nc.scalar.activation(st[:, 4:6], st[:, 7:9], ACT.Sqrt).then_inc(s_rt2, 1)
            for k in range(KT):
                act.wait_ge(s_t2, k + 1)
                nc.scalar.activation(h2T[:, k, :], ps[:, k % 2, 0:SEQ], ACT.Copy).then_inc(s_h2T, 1)

            def peer_scores(hd, hh):
                act.wait_ge(s_ps, hd + 1)
                nc.scalar.activation(sct[:, :, bass.ds(hd, 1), :].rearrange("p t a n -> p t (a n)"),
                                     ps[:, 2 + hh, :].rearrange("p (t n) -> p t n", t=TT), ACT.Copy).then_inc(s_psc, 1)

            with act.Fori(0, PH // 2) as g:
                for q in range(4):
                    n = 4 * g + q
                    act.wait_ge(s_wdone, RING + W_PQ + 1 + n)
                    nc.scalar.activation(qp[:, q % 2, :], ps[:, q % 2, 0:SEQ], ACT.Copy).then_inc(s_qp, 1)
                    if q == 2:
                        peer_scores(2 * g, 0)
                peer_scores(2 * g + 1, 1)

            def gate_exp(hd, hh):
                act.wait_ge(s_gm, hd + 1)
                nc.scalar.activation(gw[:, hh, :], tv[:, 2, :], ACT.Exp, bias=gsum[:, 0:1],
                                     accum_out=gsum[:, 1:2]).then_inc(s_gex, 1)

            for T in range(TT):
                with act.Fori(0, PH // 2) as g:
                    for hh in range(2):
                        hd = T * PH + 2 * g + hh
                        gate_exp(hd, hh)
                        for j in range(TOPK):
                            act.wait_ge(s_dot, hd * TOPK + j + 1 + UV)
                            nc.scalar.activation(ga[:, hh, j:j + 1], av[:, hh, j:j + 1], ACT.Gelu_apprx_tanh
                                                 ).then_inc(s_gl, 1)
                act.wait_ge(s_fh, T + 1)
                nc.scalar.activation(xn[:, T, :], hs2[:, T, :], ACT.Square, accum_out=st[:, 10:11]).then_inc(s_fsq, 1)
                act.wait_ge(s_frt, 2 * T + 1)
                nc.scalar.activation(st[:, 12:13], st[:, 11:12], ACT.Sqrt).then_inc(s_fsq, 1)

        @block.vector
        def _(dve):
            dve.sem_inc(s_ab, 4)
            dve.sem_inc(s_gst, 4)
            dve.sem_inc(s_oc, 4)
            dve.sem_inc(s_ye, 2)
            dve.sem_inc(s_pm, 2)
            dve.sem_inc(s_mT, 2)
            dve.sem_inc(s_hs, 4)
            dve.sem_inc(s_dot, UV)
            n_v = [0]

            def step(ins):
                n_v[0] += 1
                ins.then_inc(s_v, 1)
                dve.wait_ge(s_v, n_v[0])

            nc.vector.memset(zeros[:, :], 0.0).then_inc(s_zero, 1)
            step(nc.vector.memset(halfpi[:, :], HALF_PI))
            nc.vector.memset(st[:, :], 1.0).then_inc(s_ms, 1)
            dve.wait_ge(s_par, 16)
            d = [disc[:, k, :] for k in range(24)]
            lre, lim, ldt = col("lam_re"), col("lam_im"), col("log_dt")
            step(nc.vector.tensor_scalar(d[0], ldt, 0.125, None, ALU.mult))
            step(nc.vector.tensor_scalar(d[1], d[0], float(1 / np.prod(np.arange(1.0, 11))), None, ALU.mult))
            for k in range(9, 0, -1):
                step(nc.vector.scalar_tensor_tensor(d[1], d[1], float(1 / np.prod(np.arange(1.0, k + 1))), d[0],
                                                    ALU.add, ALU.mult))
            step(nc.vector.tensor_scalar(d[1], d[1], 1.0, None, ALU.add))
            for _ in range(3):
                step(nc.vector.tensor_tensor(d[1], d[1], d[1], ALU.mult))
            step(nc.vector.tensor_tensor(d[2], lre, d[1], ALU.mult))
            step(nc.vector.tensor_scalar(d[2], d[2], -200.0, 1.0 / 128, ALU.max, ALU.mult))
            step(nc.vector.tensor_scalar(d[3], d[2], 1.0 / 720, None, ALU.mult))
            for k in range(5, 0, -1):
                step(nc.vector.scalar_tensor_tensor(d[3], d[3], float(1 / np.prod(np.arange(1.0, k + 1))), d[2],
                                                    ALU.add, ALU.mult))
            for _ in range(7):
                step(nc.vector.scalar_tensor_tensor(d[3], d[3], 2.0, d[3], ALU.add, ALU.mult))
            step(nc.vector.tensor_tensor(d[5], lim, d[1], ALU.mult))
            step(nc.vector.tensor_scalar(d[5], d[5], float(1 / (2 * np.pi)), None, ALU.mult))
            step(nc.vector.tensor_scalar(d[8], d[5], MAGIC, None, ALU.add))
            step(nc.vector.scalar_tensor_tensor(d[9], d[8], MAGIC, d[5], ALU.subtract, ALU.subtract))
            nc.vector.tensor_scalar(d[4], d[9], -1.0, None, ALU.mult).then_inc(s_f0, 1)
            step(nc.vector.tensor_scalar(d[10], d[3], 1.0, None, ALU.add))
            dve.wait_ge(s_trig0, 2)
            step(nc.vector.scalar_tensor_tensor(d[11], d[7], -2.0, d[7], ALU.mult, ALU.mult))
            step(nc.vector.tensor_scalar(d[12], d[11], 1.0, None, ALU.add))
            step(nc.vector.tensor_tensor(d[12], d[12], d[3], ALU.mult))
            step(nc.vector.tensor_tensor(d[12], d[12], d[11], ALU.add))
            step(nc.vector.tensor_tensor(d[13], d[6], d[10], ALU.mult))
            step(nc.vector.tensor_tensor(d[14], lre, lre, ALU.mult))
            step(nc.vector.tensor_tensor(d[15], lim, lim, ALU.mult))
            step(nc.vector.tensor_tensor(d[14], d[14], d[15], ALU.add))
            step(nc.vector.reciprocal(d[14], d[14]))
            step(nc.vector.tensor_tensor(d[16], d[12], lre, ALU.mult))
            step(nc.vector.tensor_tensor(d[17], d[13], lim, ALU.mult))
            step(nc.vector.tensor_tensor(d[16], d[16], d[17], ALU.add))
            step(nc.vector.tensor_tensor(d[16], d[16], d[14], ALU.mult))
            step(nc.vector.tensor_tensor(d[18], d[13], lre, ALU.mult))
            step(nc.vector.tensor_tensor(d[19], d[12], lim, ALU.mult))
            step(nc.vector.tensor_tensor(d[18], d[18], d[19], ALU.subtract))
            step(nc.vector.tensor_tensor(d[18], d[18], d[14], ALU.mult))
            step(nc.vector.tensor_scalar(d[19], d[18], -1.0, None, ALU.mult))
            for k, a in enumerate((4, 10, 16, 18, 19)):
                nc.vector.tensor_copy(scal[:, :, k, :], d[a].rearrange("p (c i) -> p c i", i=SPC))
            for i in range(SPC):
                ins = nc.vector.tensor_copy(scal[:, :, 5, i], col("dskip"))
            step(ins)

            def rstd(dst, ss, v, root, count):
                step(nc.vector.reciprocal(dst, root))
                step(nc.vector.tensor_tensor(ss, dst, dst, ALU.mult))
                step(nc.vector.tensor_tensor(ss, ss, v, ALU.mult))
                step(nc.vector.tensor_scalar(ss, ss, -0.5, 1.5, ALU.mult, ALU.add))
                step(nc.vector.tensor_tensor(dst, dst, ss, ALU.mult))

            dve.wait_ge(s_sq, TT + 1)
            nc.vector.tensor_scalar(st[:, 7:10], st[:, 0:3], 1.0 / D, EPS, ALU.mult, ALU.add).then_inc(s_ms, 1)
            dve.wait_ge(s_ms, 2)
            dve.wait_ge(s_sqr, 1)
            rstd(st[:, 12:15], st[:, 0:3], st[:, 7:10], st[:, 4:7], 3)
            for t in range(TT):
                nc.vector.tensor_scalar(xs[:, t, :], xn[:, t, :], st[:, 12 + t:13 + t], None, ALU.mult).then_inc(s_xs, 1)
            nc.vector.tensor_scalar(xs[0:META, TT, :], xs[0:META, TT, :], st[0:META, 14:15], None, ALU.mult
                                    ).then_inc(s_xs, 1)

            def softmax_front(h, qb):
                a = 2 * h + qb
                dve.wait_ge(s_sc, a + 1)
                nc.vector.scalar_tensor_tensor(lg[:, qb, 0:L], alibi[:, qb, :], float(2.0 ** (-8.0 * (h + 1) / HEADS)),
                                               ps[:, 6 + qb, 0:L], ALU.mult, ALU.add).then_inc(s_lg, 1)
                nc.vector.tensor_copy(lg[:, qb, L:L + 1], col("sink", h, h + 1)).then_inc(s_lg, 1)
                dve.wait_ge(s_lg, 2 * a + 2)
                nc.vector.tensor_reduce(sm[:, qb, 0:1], lg[:, qb, :], AX_X, ALU.max, negate=True).then_inc(s_nm, 1)

            def softmax_back(h, qb):
                a = 2 * h + qb
                dve.wait_ge(s_pe, a + 1)
                nc.vector.reciprocal(sm[:, qb, 2:3], sm[:, qb, 1:2]).then_inc(s_al, 1)
                dve.wait_ge(s_al, a + 1)
                nc.vector.tensor_scalar(pr[:, qb, 0:L], pr[:, qb, 0:L], sm[:, qb, 2:3], None, ALU.mult).then_inc(s_pn, 1)

            def weights_T(h, qb):
                a = 2 * h + qb
                dve.wait_ge(s_pt, a + 1)
                nc.vector.tensor_copy(pT[0:META, qb, 0:P], ps[0:META, 2 + qb, 0:P]).then_inc(s_pT, 1)
                nc.vector.tensor_copy(pT[:, qb, P:3 * P], ps[:, 2 + qb, P:3 * P]).then_inc(s_pT, 1)

            def values(h, qb):
                a = 2 * h + qb
                dve.wait_ge(s_av, a + 1)
                nc.vector.tensor_copy(ybT[:, h, qb * P:(qb + 1) * P], ps[:, 4 + qb, 0:P]).then_inc(s_yb, 1)

            for h in range(HEADS):
                softmax_front(h, 0)
                softmax_back(h, 0)
                softmax_front(h, 1)
                weights_T(h, 0)
                softmax_back(h, 1)
                values(h, 0)
                weights_T(h, 1)
                values(h, 1)

            dve.wait_ge(s_uk, 2 + W_V)
            with dve.Fori(0, CT // 2) as b:
                links = [0]

                def vlink(ins):
                    links[0] += 1
                    ins.then_inc(s_vl, 1)
                    dve.wait_ge(s_vl, LINKS * b + links[0])

                def scalars(cc):
                    ct = 2 * b + cc
                    nc.vector.tensor_copy(scur[:, cc].rearrange("p k i -> p (k i)"),
                                          scal[:, bass.ds(ct, 1), :, :].rearrange("p a k i -> p (a k i)")
                                          ).then_inc(s_scur, 1)
                    nc.vector.tensor_copy(ucur[:, cc, :], flat(ukT[:, bass.ds(ct, 1), :])).then_inc(s_scur, 1)
                    dve.wait_ge(s_scur, 2 * ct + 2)

                def angles(t):
                    if t % SPC == 0:
                        scalars(t // SPC)
                    s = t % 2
                    vlink(nc.vector.tensor_scalar(tb[:, 0, :], iota, scur[:, t // SPC, 0, t % SPC:t % SPC + 1], None,
                                                  ALU.mult))
                    vlink(nc.vector.tensor_scalar(tb[:, 1, :], tb[:, 0, :], MAGIC, None, ALU.add))
                    vlink(nc.vector.scalar_tensor_tensor(ang[:, s, 0, :], tb[:, 1, :], MAGIC, tb[:, 0, :],
                                                         ALU.subtract, ALU.subtract))
                    nc.vector.scalar_tensor_tensor(ang[:, s, 1, :], ang[:, s, 0, :], -1.0, ang[:, s, 0, :],
                                                   ALU.mult, ALU.max).then_inc(s_ang, 1)

                def input_products(t):
                    s, n = t % 2, RPL * b + t
                    dve.wait_ge(s_trg, 2 * n + 2)
                    dve.wait_ge(s_bu, n + 17)
                    bu = ps[:, 2 + 2 * s:4 + 2 * s, 0:L]
                    cos = trig[:, t % 4, 0:1, :].broadcast_to([P, 2, L])
                    nc.vector.tensor_tensor(pa[:, s], bu, cos, ALU.mult).then_inc(s_ab, 1)
                    sin = trig[:, t % 4, 1:2, :].broadcast_to([P, 2, L])
                    nc.vector.tensor_tensor(pb[:, s], ps[:, 3 + 2 * s:1 + 2 * s:-1, 0:L], sin, ALU.mult).then_inc(s_ab, 1)

                def scans(t):
                    s, n = t % 2, RPL * b + t
                    dve.wait_ge(s_gin, 2 * n + 2)
                    dve.wait_ge(s_os, n + 3)
                    r = scur[:, t // SPC, 1, t % SPC:t % SPC + 1].broadcast_to([P, L])
                    for k in range(2):
                        nc.vector.tensor_tensor_scan(gst[:, s, k, :], r, gin[:, s, k, :], 0.0, ALU.mult, ALU.add
                                                     ).then_inc(s_gst, 1)
                    dve.wait_ge(s_gst, 2 * n + 6)
                    dve.wait_ge(s_y, n + 15)
                    nc.vector.tensor_tensor(oc[:, s], trig[:, t % 4, 0:1, :].broadcast_to([P, 2, L]), gst[:, s],
                                            ALU.mult).then_inc(s_oc, 1)

                def take_y(cc):
                    ct = 2 * b + cc
                    dve.wait_ge(s_y, SPC * ct + SPC + 16)
                    nc.vector.scalar_tensor_tensor(flat(yT[:, bass.ds(ct, 1), :]), ucur[:, cc, META:L],
                                                   scur[:, cc, 5, 0:1], ps[:, 6 + cc, 0:SEQ], ALU.mult, ALU.add
                                                   ).then_inc(s_ye, 1)

                LINKS = 3 * RPL
                angles(0)
                for t in range(RPL):
                    if t + 1 < RPL:
                        angles(t + 1)
                    input_products(t)
                    if t >= 1:
                        scans(t - 1)
                    if t == SPC + 2:
                        take_y(0)
                scans(RPL - 1)
                take_y(1)
                assert links[0] == LINKS

            dve.wait_ge(s_gel, 1)
            for m in range(CT):
                dve.wait_ge(s_sig, m + 1)
                nc.vector.tensor_tensor(yaT[:, m, :], yT[:, m, :], qT[:, m % 2, :], ALU.mult).then_inc(s_ya, 1)
            dve.wait_ge(s_sgg, 1)
            with dve.Fori(0, KT // 4) as i:
                for q in range(4):
                    dve.wait_ge(s_wdone, RING + W_PROJ + 1 + q + 4 * i)
                    dve.wait_ge(s_mT, 1 + q + 4 * i)
                    nc.vector.tensor_tensor(pa[:, q % 2, :, 0:SEQ], gt[:, :, bass.ds(q + 4 * i, 1), :].rearrange("p b a t -> p b (a t)"),
                                            ps[:, q % 2, :].rearrange("p (b t) -> p b t", b=2), ALU.mult).then_inc(s_pm, 1)
                    dve.wait_ge(s_pm, 3 + q + 4 * i)
                    nc.vector.tensor_tensor(flat(mT[:, bass.ds(q + 4 * i, 1), :]), pa[:, q % 2, 0, 0:SEQ],
                                            pa[:, q % 2, 1, 0:SEQ], ALU.add).then_inc(s_mT, 1)
            with dve.Fori(0, 2) as i:
                for q in range(2):
                    for T in range(TT):
                        dve.wait_ge(s_wdone, RING + W_OUT + 4 * q + 4 + 8 * i)
                        nc.vector.tensor_tensor(hs2[:, T, bass.ds(512 * q + 1024 * i, 512)], ps[:, 2 * q + T, :],
                                                xn[:, T, bass.ds(512 * q + 1024 * i, 512)], ALU.add).then_inc(s_hs, 1)
            nc.vector.memset(st[:, 0:2], 1.0).then_inc(s_ms2, 1)
            dve.wait_ge(s_sq2, TT)
            nc.vector.tensor_scalar(st[:, 7:9], st[:, 0:2], 1.0 / D, EPS, ALU.mult, ALU.add).then_inc(s_ms2, 1)
            dve.wait_ge(s_rt2, 1)
            dve.wait_ge(s_ms2, 2)
            rstd(st[:, 12:14], st[:, 0:2], st[:, 7:9], st[:, 4:6], 2)
            dve.wait_ge(s_gbd, 16)
            for T in range(TT):
                nc.vector.scalar_tensor_tensor(xn[:, T, :], hs2[:, T, :], st[:, 12 + T:13 + T], gb[:, 0, :],
                                               ALU.mult, ALU.mult).then_inc(s_h2, 1)

            def top16(vals, idxs, src, spare):
                yield nc.vector.max(vals[:, 0:8], src)
                yield nc.vector.max_index(idxs[:, 0:8], vals[:, 0:8], src)
                yield nc.vector.match_replace(spare, vals[:, 0:8], src, NEG)
                yield nc.vector.max(vals[:, 8:16], spare)
                yield nc.vector.max_index(idxs[:, 8:16], vals[:, 8:16], spare)

            TK = 31

            def select(T, g, hh, base):
                hd = T * PH + 2 * g + hh
                k = [0]

                def tl(ins):
                    k[0] += 1
                    ins.then_inc(s_tk, 1)
                    dve.wait_ge(s_tk, base + k[0])
                    dve.sem_inc(s_lonev, 1)

                tl(nc.vector.tensor_copy(ks[:, :], sct[:, T, bass.ds(2 * g + hh, 1), :].rearrange("p a n -> p (a n)")))
                for s in range(2):
                    for ins in top16(tv[:, s, :], ti[:, s, :], ks[:, s * NK:(s + 1) * NK], kr[:, s * NK:(s + 1) * NK]):
                        tl(ins)
                    tl(nc.vector.tensor_copy(tif[:, s, :], ti[:, s, :]))

                def rows(ap):
                    return ap.rearrange("p (a o) -> p a o", o=1).broadcast_to([P, TOPK, TOPK])

                def cols_(ap):
                    return ap.rearrange("p (o a) -> p o a", o=1).broadcast_to([P, TOPK, TOPK])
                tl(nc.vector.tensor_tensor(cand[:, :, :], rows(tv[:, 0, :]), cols_(tv[:, 1, :]), ALU.add))
                cf, of = cand[:, :, :].rearrange("p a b -> p (a b)"), oh[:, :, :].rearrange("p a b -> p (a b)")
                for ins in top16(tv[:, 2, :], ti[:, 2, :], cf, of):
                    tl(ins)
                nc.vector.tensor_scalar(gsum[:, 0:1], tv[:, 2, 0:1], -1.0, None, ALU.mult).then_inc(s_gm, 1)
                tl(nc.vector.tensor_scalar(tq[:, 0, :], ti[:, 2, :], 4, None, ALU.logical_shift_right))
                tl(nc.vector.tensor_scalar(tq[:, 1, :], ti[:, 2, :], TOPK - 1, None, ALU.bitwise_and))
                for s in range(2):
                    tl(nc.vector.tensor_copy(tif[:, 2 + s, :], tq[:, s, :]))
                    tl(nc.vector.tensor_tensor(oh[:, :, :], rows(tif[:, 2 + s, :]), cols_(col("iota16")), ALU.is_equal))
                    tl(nc.vector.tensor_tensor(oh[:, :, :], oh[:, :, :], cols_(tif[:, s, :]), ALU.mult))
                    tl(nc.vector.tensor_reduce(tif[:, 2 + s, :], oh[:, :, :], AX_X, ALU.add))
                nc.vector.scalar_tensor_tensor(eid[:, hh, :], tif[:, 2, :], float(NK), tif[:, 3, :], ALU.mult, ALU.add
                                               ).then_inc(s_eid, 1)
                dve.wait_ge(s_gex, hd + 1)
                tl(nc.vector.reciprocal(gsum[:, 2:3], gsum[:, 1:2]))
                tl(nc.vector.tensor_scalar(gw[:, hh, :], gw[:, hh, :], gsum[:, 2:3], None, ALU.mult))
                assert k[0] == TK, k[0]

            dve.wait_ge(s_psc, 2 + PH)
            for T in range(TT):
                with dve.Fori(0, PH // 2) as g:
                    def diag(hh, j):
                        m = (T * PH + 2 * g + hh) * TOPK + j
                        dve.wait_ge(s_gl, m + 1)
                        dve.wait_ge(s_ex, m + 1 + (UV - 2))
                        nc.vector.tensor_scalar(dg[:, j % 2, :], ident, ga[:, hh, j:j + 1], gw[:, hh, j:j + 1],
                                                ALU.mult, ALU.mult).then_inc(s_dg, 1)

                    for hh in range(2):
                        select(T, g, hh, TK * (T * PH + hh) + 2 * TK * g)
                        for j in range(TOPK):
                            m = (T * PH + 2 * g + hh) * TOPK + j
                            dve.wait_ge(s_u[j % UV], 16 * ((T * PH + hh) * (TOPK // UV) + j // UV + 1) + 16 * 2 * (TOPK // UV) * g)
                            nc.vector.tensor_tensor_reduce(uv[:, j % UV, 0, :], uv[:, j % UV, 0, :], xn[:, T, :], 1.0, 0.0,
                                                           ALU.mult, ALU.add, av[:, hh, j:j + 1]).then_inc(s_dot, 1)
                            if j >= 1:
                                diag(hh, j - 1)
                        diag(hh, TOPK - 1)
                dve.wait_ge(s_acc, T + 1)
                nc.vector.tensor_copy(hs2[:, T, :], ps[:, 4 * T:4 * T + 4, :].rearrange("p b n -> p (b n)")).then_inc(s_fh, 1)
                dve.wait_ge(s_fsq, 2 * T + 1)
                nc.vector.tensor_scalar(st[:, 11:12], st[:, 10:11], 1.0 / D, EPS, ALU.mult, ALU.add).then_inc(s_frt, 1)
                dve.wait_ge(s_frt, 2 * T + 1)
                dve.wait_ge(s_fsq, 2 * T + 2)
                rstd(st[:, 13:14], st[:, 14:15], st[:, 11:12], st[:, 12:13], 1)
                dve.wait_ge(s_kd, 32)
                nc.vector.scalar_tensor_tensor(xn[:, T, :], hs2[:, T, :], st[:, 13:14], gb[:, 1, :], ALU.mult, ALU.mult
                                               ).then_inc(s_frt, 1)
                dve.wait_ge(s_frt, 2 * T + 2)
                dve.sem_inc(s_fin, 1)

        @block.tensor
        def _(pe):
            pe.sem_inc(s_wdone, RING)
            pe.sem_inc(s_bu, 16)
            pe.sem_inc(s_y, 16)
            pe.sem_inc(s_ex, UV)

            def weights_in(n0, i=0):
                pe.wait_ge(s_w[n0 % RING], 16 * (n0 // RING + 1) + 16 * i)

            def product(dst, n0, rhs, kts=KT, block0=0, m=KT, k0=0):
                w = wtile(n0, m, P)
                for k in range(kts):
                    ins = nc.tensor.matmul(dst, w[:, block0 + k, :], rhs(k0 + k), start=(k == 0), stop=(k == kts - 1))
                return ins

            pe.wait_ge(s_par, 16)
            pe.wait_ge(s_xs, TT + 1)
            for k in range(KT):
                pe.wait_ge(s_hT, k + 1)
                c = slice(k * P, (k + 1) * P)
                nc.tensor.transpose(ps[:, k % 2, 0:META], xs[0:META, TT, c], ident[0:META, 0:META])
                for t in range(TT):
                    ins = nc.tensor.transpose(ps[:, k % 2, META + t * P:META + (t + 1) * P], xs[:, t, c], ident)
                ins.then_inc(s_tr, 1)
            pe.wait_ge(s_hT, 2 + KT)
            for m in range(W_V):
                weights_in(m)
                pe.wait_ge(s_uk, m + 1)
                product(ps[:, m % 2, 0:L], m, lambda k: hTv[:, k, :]).then_inc(s_wdone, 1)
            weights_in(W_V)
            weights_in(W_V + 1)
            for t in range(TT + 1):
                rows, c = (P, slice(META + t * P, META + (t + 1) * P)) if t < TT else (META, slice(0, META))
                for k in range(KT):
                    w = wtile(W_V + k // 8, 8, KVH * HD)
                    ins = nc.tensor.matmul(ps[0:rows, 2 + t, 0:KVH * HD], hTv[:, k, c], w[:, k % 8, :],
                                           start=(k == 0), stop=(k == KT - 1))
                ins.then_inc(*((s_vp, 1) if t < TT else (s_wdone, 2)))

            def queries(h, part):
                n = W_Q + h
                if part == 0:
                    weights_in(n)
                    if h >= 2:
                        pe.wait_ge(s_qT[h % 2], h // 2 + 1)
                w = wtile(n, KT, P)
                for k in range(8 * part, 8 * part + 8):
                    ins = nc.tensor.matmul(ps[:, h % 2, 0:SEQ], w[:, k, :], hTv[:, k, META:L],
                                           start=(k == 0), stop=(k == KT - 1))
                if part:
                    ins.then_inc(s_wdone, 1)

            def scores(h, qb):
                a = 2 * h + qb
                if qb == 0:
                    pe.wait_ge(s_qT[h % 2], h // 2 + 2)
                if a >= 2:
                    pe.wait_ge(s_lg, 2 * (a - 2) + 1)
                nc.tensor.matmul(ps[:, 6 + qb, 0:L], qT[:, h % 2, qb * P:(qb + 1) * P], ukT[:, CT + h // 4, :],
                                 start=True, stop=True).then_inc(s_sc, 1)

            def transposes(h, qb):
                a = 2 * h + qb
                pe.wait_ge(s_pn, a + 1)
                if a >= 2:
                    pe.wait_ge(s_pT, 2 * (a - 1))
                if a == 0:
                    pe.wait_ge(s_ve, TT + 1)
                b0 = ps[:, 2 + qb, :]
                nc.tensor.transpose(b0[0:META, 0:P], pr[:, qb, 0:META], ident)
                for t in range(TT):
                    ins = nc.tensor.transpose(b0[:, (t + 1) * P:(t + 2) * P], pr[:, qb, META + t * P:META + (t + 1) * P], ident)
                ins.then_inc(s_pt, 1)

            def values(h, qb):
                a = 2 * h + qb
                kv = slice(h // 4 * HD, (h // 4 + 1) * HD)
                pe.wait_ge(s_pT, 2 * a + 2)
                if a >= 2:
                    pe.wait_ge(s_yb, a - 1)
                o = ps[:, 4 + qb, 0:P]
                nc.tensor.matmul(o, vr[:, 0, kv], pT[:, qb, P:2 * P], start=True, stop=False)
                nc.tensor.matmul(o, vr[:, 1, kv], pT[:, qb, 2 * P:3 * P], start=False, stop=False)
                nc.tensor.matmul(o, vm[:, kv], pT[0:META, qb, 0:P], start=False, stop=True).then_inc(s_av, 1)

            pe.wait_ge(s_uk, 2 + W_V)
            queries(0, 0)
            queries(0, 1)
            for h in range(HEADS):
                scores(h, 0)
                if h + 1 < HEADS:
                    queries(h + 1, 0)
                transposes(h, 0)
                scores(h, 1)
                if h + 1 < HEADS:
                    queries(h + 1, 1)
                values(h, 0)
                transposes(h, 1)
                values(h, 1)

            pe.wait_ge(s_yb, 2 * HEADS)
            pe.wait_ge(s_pT, 4 * HEADS)
            with pe.Fori(0, CT // 2) as b:
                def state_inputs(t):
                    s, n, cc, j, way = t % 2, RPL * b + t, t // SPC, t % SPC // 2, t % 2
                    if t % SPC == 0:
                        pe.wait_ge(s_bw[cc], 16 * b + 16)
                        pe.wait_ge(s_scur, 2 * (2 * b + cc) + 2)
                    pe.wait_ge(s_ab, 2 * n + 2)
                    rows = slice(32 * j, 32 * j + 32)
                    u = ucur[rows, cc, :]
                    if way:
                        u = u[:, L - 1::-1]
                    for r in range(2):
                        ins = nc.tensor.matmul(ps[:, 2 + 2 * s + r, 0:L], bwt[rows, cc, way, r, :], u, start=True, stop=True)
                    ins.then_inc(s_bu, 1)

                def half_gate(t):
                    q = t // 2
                    g = SPC * b + q
                    if t % 2 == 0:
                        weights_in(W_GATE + q, 2 * b)
                        pe.wait_ge(s_gs, g + 1)
                    w = wtile(W_GATE + q, KT, P)
                    for k in range(8 * (t % 2), 8 * (t % 2) + 8):
                        ins = nc.tensor.matmul(ps[:, q % 2, 0:SEQ], w[:, k, :], hTv[:, k, META:L],
                                               start=(k == 0), stop=(k == KT - 1))
                    if t % 2:
                        ins.then_inc(s_wdone, 1)

                def state_outputs(t):
                    s, n, cc, i = t % 2, RPL * b + t, t // SPC, t % SPC
                    j, way = i // 2, i % 2
                    pe.wait_ge(s_oc, n + 5)
                    pe.wait_ge(s_os, n + 5)
                    if i == 0:
                        pe.wait_ge(s_cp, 3 * (2 * b + cc) + 9)
                        pe.wait_ge(s_ye, 2 * b + cc + 1)
                    dst = ps[32 * j:32 * j + 32, 6 + cc, 0:SEQ]
                    span = slice(SEQ - 1, None, -1) if way else slice(META, L)
                    terms = ((0, oc[:, s, 0]), (1, os_[:, s, 1]), (2, oc[:, s, 1]), (2, os_[:, s, 0]))
                    for k, (c, rhs) in enumerate(terms):
                        ins = nc.tensor.matmul(dst, cp[:, cc, c, i, :], rhs[:, span], start=(way == 0 and k == 0),
                                               stop=(way == 1 and k == 3))
                    ins.then_inc(s_y, 1)

                for t in range(RPL):
                    state_inputs(t)
                    half_gate(t)
                    if t >= 1:
                        state_outputs(t - 1)
                state_outputs(RPL - 1)

            pe.wait_ge(s_gel, 1)
            pe.wait_ge(s_gs, 2 + GATES)
            for m in range(CT):
                if m % 2 == 0:
                    weights_in(W_GLU + m // 2)
                if m >= 2:
                    pe.wait_ge(s_sig, m - 1)
                product(ps[:, m % 2, 0:SEQ], W_GLU + m // 2, lambda k: yT[:, k, :], kts=CT, block0=CT * (m % 2)
                        ).then_inc(*((s_glu, 1) if m % 2 == 0 else (s_wdone, 1)))
            pe.wait_ge(s_ya, CT)
            with pe.Fori(0, KT // 4) as i:
                for q in range(4):
                    weights_in(W_PROJ + q, i)
                    pe.wait_ge(s_pm, 1 + q + 4 * i)
                    product(ps[:, q % 2, 0:SEQ], W_PROJ + q, lambda k: yaT[:, k, :], kts=CT)
                    product(ps[:, q % 2, SEQ:2 * SEQ], W_PROJ + q, lambda k: ybT[:, k, :], kts=HEADS, block0=CT
                            ).then_inc(s_wdone, 1)
            pe.wait_ge(s_mT, KT + 2)
            with pe.Fori(0, 2) as i:
                for q in range(2):
                    pe.wait_ge(s_hs, 2 * q + 2 + 4 * i)
                    for g in range(4):
                        n = W_OUT + 4 * q + g
                        weights_in(n, 2 * i)
                        w = wtile(n, 4, 512)
                        for kk in range(4):
                            k = 4 * g + kk
                            for T in range(TT):
                                ins = nc.tensor.matmul(ps[:, 2 * q + T, :], mT[:, k, T * P:(T + 1) * P], w[:, kk, :],
                                                       start=(k == 0), stop=(k == KT - 1))
                        ins.then_inc(s_wdone, 1)
            pe.wait_ge(s_h2, TT)
            for k in range(KT):
                pe.wait_ge(s_h2T, k + 1)
                for T in range(TT):
                    ins = nc.tensor.transpose(ps[:, k % 2, T * P:(T + 1) * P], xn[:, T, k * P:(k + 1) * P], ident)
                ins.then_inc(s_t2, 1)
            pe.wait_ge(s_h2T, 2 + KT)
            pe.wait_ge(s_kd, 32)

            with pe.Fori(0, PH // 2) as g:
                def peer_scores(q):
                    hh, half = q // 2, q % 2
                    pe.wait_ge(s_qp, 3 + q + 4 * g)
                    if half == 0:
                        pe.wait_ge(s_psc, 1 + hh + 2 * g)
                    for T in range(TT):
                        ins = nc.tensor.matmul(ps[:, 2 + hh, T * 2 * NK + half * NK:T * 2 * NK + (half + 1) * NK],
                                               qp[:, half, T * P:(T + 1) * P],
                                               keyt[:, bass.ds(2 * g + hh, 1), half, :].rearrange("p a n -> p (a n)"),
                                               start=True, stop=True)
                    if half:
                        ins.then_inc(s_ps, 1)

                for q in range(4):
                    weights_in(W_PQ + q, g)
                    pe.wait_ge(s_qp, 1 + q + 4 * g)
                    product(ps[:, q % 2, 0:SEQ], W_PQ + q, lambda k: h2T[:, k, :]).then_inc(s_wdone, 1)
                    if q >= 1:
                        peer_scores(q - 1)
                peer_scores(3)

            pe.wait_ge(s_zero, 1)
            pe.wait_ge(s_psc, 2 + PH)
            for T in range(TT):
                acc = [ps[:, 4 * T + n, :] for n in range(4)]
                for n in range(4):
                    nc.tensor.matmul(acc[n], zeros[:, 0:P], zeros[:, P:P + 512], start=True, stop=False, skip_group_check=True)
                with pe.Fori(0, PH // 2) as g:
                    for hh in range(2):
                        for j in range(TOPK):
                            m = (T * PH + 2 * g + hh) * TOPK + j
                            pe.wait_ge(s_dg, m + 1)
                            pe.wait_ge(s_vv[j % UV], 16 * ((T * PH + hh) * (TOPK // UV) + j // UV + 1) + 16 * 2 * (TOPK // UV) * g)
                            for n in range(4):
                                ins = nc.tensor.matmul(acc[n], dg[:, j % 2, :], uv[:, j % UV, 1, n * 512:(n + 1) * 512],
                                                       start=False, stop=False, skip_group_check=True)
                            ins.then_inc(s_ex, 1)
                for n in range(4):
                    ins = nc.tensor.matmul(acc[n], ident, hs2[:, T, n * 512:(n + 1) * 512], start=False, stop=True,
                                           skip_group_check=True)
                ins.then_inc(s_acc, 1)


def lay_out(a):
    f = lambda n: np.asarray(a[n], np.float32) if np.asarray(a[n]).dtype != np.float32 else np.asarray(a[n])
    w_in = f("w_in")[0]

    def tiles(w):
        k, n = w.shape
        return w.reshape(k // P, P, n // P, P).transpose(2, 1, 0, 3).reshape(n // P, P, k)

    def rows(w, c):
        k, n = w.shape
        m = D // c
        return w.reshape(k // P // m, m, P, n // c, c).transpose(3, 0, 2, 1, 4).reshape(-1, P, D)

    q0, k0, v0, g0 = SSM_W, SSM_W + HEADS * HD, SSM_W + HEADS * HD + KVH * HD, SSM_W + HEADS * HD + 2 * KVH * HD
    glu = tiles(f("ssm_w_glu")[0]).reshape(CT // 2, 2, P, SSM_W).transpose(0, 2, 1, 3).reshape(CT // 2, P, D)
    proj = np.concatenate([tiles(f("w_proj_ssm")[0]), tiles(f("w_proj_attn")[0])], axis=2)
    W = np.concatenate([tiles(w_in[:, 0:q0]), tiles(w_in[:, k0:v0]), rows(w_in[:, v0:g0], KVH * HD),
                        tiles(w_in[:, q0:k0]), tiles(w_in[:, g0:]), glu, proj, rows(f("w_out")[0], 512),
                        tiles(f("peer_w_q")[0])])
    assert W.shape == (W_END, P, D), W.shape
    keys = np.stack([f("peer_k1")[0], f("peer_k2")[0]]).transpose(3, 1, 0, 2).reshape(P, PH * 2 * NK)

    def states(v):
        return v.reshape(2, CT, SPC // 2, 2, ST).transpose(3, 4, 1, 2, 0).reshape(P, NST)

    def column(v, n):
        return v.reshape(n, P).T

    t = np.arange(SEQ)
    dist = np.abs(t[:, None] - t[None, :]).astype(np.float32)
    bias = np.where(dist <= WINDOW, -dist, np.float32(-1e30)).astype(np.float32)
    alibi = np.concatenate([np.zeros((SEQ, META), np.float32), bias], 1).reshape(TT, P, L).transpose(1, 0, 2).reshape(P, TT * L)
    ldt = np.broadcast_to(f("ssm_log_dt")[0][:, :, None], (2, GROUPS, ST))
    par = np.concatenate([
        column(f("norm_mix")[0], KT), column(f("b_gate")[0], GATES), column(f("ssm_d")[0], CT),
        column(f("ssm_b_glu")[0], CT), np.broadcast_to(f("attn_sink")[0], (P, HEADS)),
        states(f("ssm_lam_re")[0]), states(f("ssm_lam_im")[0]), states(ldt),
        np.broadcast_to(np.arange(L, dtype=np.float32), (P, L)), np.eye(P, dtype=np.float32), alibi,
        np.broadcast_to(np.arange(TOPK, dtype=np.float32), (P, TOPK))], axis=1)
    bw = np.zeros((CT, SPC // 2, 2, GC, 2, 2, 2, ST), np.float32)
    cw = np.zeros((CT, 2, ST, SPC // 2, 2, 2, 2, GC), np.float32)
    for r, (bn, cn) in enumerate((("ssm_b_re", "ssm_c_re"), ("ssm_b_im", "ssm_c_im"))):
        bv = f(bn)[0].reshape(2, CT, SPC // 2, 2, ST, GC)
        cv = f(cn)[0].reshape(2, CT, SPC // 2, 2, GC, ST)
        for g in range(2):
            bw[:, :, g, :, :, r, g, :] = bv[:, :, :, g].transpose(1, 2, 4, 0, 3)
            cw[:, g, :, :, :, r, g, :] = cv[:, :, :, g].transpose(1, 4, 2, 0, 3)
    return {
        "W": W, "keys": keys, "par": par, "bw": bw.reshape(CT, P, 4 * P), "cw": cw.reshape(CT, P, SPC * 64),
        "meta": f("meta_tokens"), "x": f("x")[0], "gffn": np.broadcast_to(f("norm_ffn")[0], (P, D)),
        "gfin": np.broadcast_to(f("norm_final"), (P, D)), "u_tab": f("peer_u")[0], "v_tab": f("peer_v")[0],
    }


ORDER = ["W", "keys", "par", "bw", "cw", "meta", "x", "gffn", "gfin", "u_tab", "v_tab"]


def kernel(**inputs):
    import concourse.bacc as bacc
    from concourse.bass_utils import run_bass_kernel_spmd

    nc = bacc.Bacc("TRN2", target_bir_lowering=False, num_devices=1)
    laid = lay_out(inputs)
    arrays = {n: np.ascontiguousarray(laid[n]) for n in ORDER}
    aps = [nc.dram_tensor(n, arrays[n].shape, F32, kind="ExternalInput").ap() for n in ORDER]
    out = nc.dram_tensor("out", (SEQ, D), F32, kind="ExternalOutput").ap()
    build(nc, *aps, out)
    r = run_bass_kernel_spmd(nc, [arrays], core_ids=[0])
    return r.results[0]["out"].reshape(1, SEQ, D)
```

```python
from contextlib import ExitStack

import concourse.bass as bass
from concourse import mybir
import numpy as np

F32 = mybir.dt.float32
U32 = mybir.dt.uint32
ALU = mybir.AluOpType
ACT = mybir.ActivationFunctionType
AX_X = mybir.AxisListType.X

P = 128
D = 2048
KT = D // P
META, SEQ = 16, 256
L = META + SEQ
TT = SEQ // P
SSM_W, GROUPS, GC, ST = 1024, 64, 16, 64
CT = SSM_W // P
NST = 2 * GROUPS * ST // P
SPC = NST // CT
HEADS, KVH, HD = 8, 2, 128
WINDOW = 128
GATES = 2 * D // P
PH, NK, TOPK = 8, 128, 16
EPS = 1e-6
RING = 4
NEG = -3.0e38
MAGIC = 1.5 * 2.0 ** 23
TWO_PI = 6.283185
HALF_PI = float(np.pi / 2)
UV = 4

W_UK, W_V, W_Q, W_GATE, W_GLU, W_PROJ, W_OUT, W_PQ, W_END = 0, 10, 12, 20, 52, 56, 72, 88, 104

COLS, _at = {}, 0
for _name, _n in (("gmix", KT), ("bgate", GATES), ("dskip", CT), ("bglu", CT), ("sink", HEADS),
                  ("lam_re", NST), ("lam_im", NST), ("log_dt", NST), ("iota", L), ("ident", P),
                  ("alibi", TT * L), ("iota16", TOPK), ("gffn", KT)):
    COLS[_name] = (_at, _at + _n)
    _at += _n
NPAR = _at
NSC = 6


def build(nc, W, keys, par, bw, cw, meta, x, gffn, gfin, u_tab, v_tab, out):
    top = ExitStack()
    with top:
        def sem(name):
            return top.enter_context(nc.semaphore(name))

        def sbt(stack, name, shape, dt=F32):
            return stack.enter_context(nc.sbuf_tensor(name, shape, dt))

        prm = sbt(top, "prm", [P, NPAR])
        ring = sbt(top, "ring", [P, RING, D])
        xn = sbt(top, "xn", [P, TT, D])
        hs2 = sbt(top, "hs2", [P, TT, D])
        st = sbt(top, "st", [P, 16])
        halfpi = sbt(top, "halfpi", [P, 1])

        mix = ExitStack()
        hT = sbt(mix, "hT", [P, KT * L])
        ukT = sbt(mix, "ukT", [P, 10, L])
        vm = sbt(mix, "vm", [META, KVH * HD])
        vr = sbt(mix, "vr", [P, TT, KVH * HD])
        ybT = sbt(mix, "ybT", [P, HEADS, SEQ])
        yT = sbt(mix, "yT", [P, CT, SEQ])
        gates = sbt(mix, "gates", [P, GATES * SEQ])
        qT = sbt(mix, "qT", [P, 2, SEQ])
        pr = sbt(mix, "pr", [P, 2, L + 1])
        pT = sbt(mix, "pT", [P, 2, 3 * P])
        sm = sbt(mix, "sm", [P, 2, 4])
        scal = sbt(mix, "scal", [P, CT, NSC, SPC])
        scur = sbt(mix, "scur", [P, 2, NSC, SPC])
        ucur = sbt(mix, "ucur", [P, 2, L])
        bwt = sbt(mix, "bwt", [P, 2, 2, 2, P])
        cwt = sbt(mix, "cwt", [P, 2, SPC, 2, 32])
        cp = sbt(mix, "cp", [P, 2, 2, SPC, 32])
        cs = sbt(mix, "cs", [P, 4, SPC, 32])
        tb = sbt(mix, "tb", [P, 3, L])
        ang = sbt(mix, "ang", [P, 2, 2, L])
        trig = sbt(mix, "trig", [P, 4, 2, L])
        pa = sbt(mix, "pa", [P, 2, 2, L])
        pb = sbt(mix, "pb", [P, 2, 2, L])
        gin = sbt(mix, "gin", [P, 2, 2, L])
        mix.close()
        h2f = hs2[:, :, :].rearrange("p t d -> p (t d)")

        def in_hs2(at):
            return h2f[:, at * 4 * L:(at + 1) * 4 * L].rearrange("p (s r t) -> p s r t", s=2, r=2)
        gst, oc, os_ = in_hs2(0), in_hs2(1), in_hs2(2)
        lg = h2f[:, 12 * L:12 * L + 2 * (L + 1)].rearrange("p (s t) -> p s t", s=2)
        disc = gates[:, 3 * D:3 * D + 24 * NST].rearrange("p (k n) -> p k n", k=24)
        xs = gates[:, 0:3 * D].rearrange("p (t d) -> p t d", t=3)
        hTv = hT[:, :].rearrange("p (k t) -> p k t", k=KT)
        mT = hT[:, 0:KT * SEQ].rearrange("p (k t) -> p k t", k=KT)
        yaT = ukT[:, :, :].rearrange("p a t -> p (a t)")[:, 0:CT * SEQ].rearrange("p (k t) -> p k t", k=CT)
        gt = gates[:, :].rearrange("p (b k t) -> p b k t", b=2, k=KT)

        exp_ = ExitStack()
        uv = sbt(exp_, "uv", [P, UV, 2, D])
        h2T = sbt(exp_, "h2T", [P, KT, SEQ])
        sct = sbt(exp_, "sct", [P, TT * PH, 2 * NK])
        keyt = sbt(exp_, "keyt", [P, PH, 2, NK])
        gb = sbt(exp_, "gb", [P, 2, D])
        qp = sbt(exp_, "qp", [P, 2, SEQ])
        dg = sbt(exp_, "dg", [P, 2, P])
        ks = sbt(exp_, "ks", [P, 2 * NK])
        kr = sbt(exp_, "kr", [P, 2 * NK])
        tv = sbt(exp_, "tv", [P, 3, TOPK])
        ti = sbt(exp_, "ti", [P, 3, TOPK], U32)
        tif = sbt(exp_, "tif", [P, 4, TOPK])
        tq = sbt(exp_, "tq", [P, 2, TOPK], U32)
        cand = sbt(exp_, "cand", [P, TOPK, TOPK])
        oh = sbt(exp_, "oh", [P, TOPK, TOPK])
        eid = sbt(exp_, "eid", [P, 2, TOPK], U32)
        gw = sbt(exp_, "gw", [P, 2, TOPK])
        gsum = sbt(exp_, "gsum", [P, 4])
        av = sbt(exp_, "av", [P, 2, TOPK])
        ga = sbt(exp_, "ga", [P, 2, TOPK])
        exp_.close()

        ps = top.enter_context(nc.psum_tensor("ps", [P, 8, 512], F32))

        def col(name, a=0, b=None):
            lo, hi = COLS[name]
            return prm[:, lo + a:hi if b is None else lo + b]

        ident = col("ident")
        iota = col("iota")
        alibi = col("alibi").rearrange("p (b t) -> p b t", b=TT)

        def wtile(n, m, c):
            return ring[:, n % RING, :].rearrange("p (m c) -> p m c", m=m, c=c)

        s_par = sem("s_par")
        s_x = [sem(f"s_x{t}") for t in range(TT + 1)]
        s_w = [sem(f"s_w{i}") for i in range(RING)]
        s_wdone = sem("s_wdone")
        s_v = sem("s_v")
        s_tr = sem("s_tr")
        s_trig0, s_f0 = sem("s_trig0"), sem("s_f0")
        s_sq, s_ms, s_sqr, s_xs = sem("s_sq"), sem("s_ms"), sem("s_sqr"), sem("s_xs")
        s_hT = sem("s_hT")
        s_uk = sem("s_uk")
        s_vp, s_ve = sem("s_vp"), sem("s_ve")
        s_qT = [sem("s_qT0"), sem("s_qT1")]
        s_sc, s_lg, s_nm, s_pe, s_pn, s_pt, s_pT, s_av, s_yb = (
            sem(n) for n in ("s_sc", "s_lg", "s_nm", "s_pe", "s_pn", "s_pt", "s_pT", "s_av", "s_yb"))
        s_al = sem("s_al")
        s_bw = [sem("s_bw0"), sem("s_bw1")]
        s_cw = [sem("s_cw0"), sem("s_cw1")]
        s_scur, s_cpl = sem("s_scur"), sem("s_cpl")
        s_cp = sem("s_cp")
        s_bu = sem("s_bu")
        s_vl = sem("s_vl")
        s_tb, s_trg = sem("s_tb"), sem("s_trg")
        s_ang = sem("s_ang")
        s_ab = sem("s_ab")
        s_gin = sem("s_gin")
        s_gst = sem("s_gst")
        s_oc, s_os = sem("s_oc"), sem("s_os")
        s_re, s_im = sem("s_re"), sem("s_im")
        s_y = sem("s_y")
        s_ye = sem("s_ye")
        s_gs = sem("s_gs")
        s_gel, s_sgg, s_glu, s_sig, s_ya = sem("s_gel"), sem("s_sgg"), sem("s_glu"), sem("s_sig"), sem("s_ya")
        s_pm, s_mT = sem("s_pm"), sem("s_mT")
        s_hs = sem("s_hs")
        s_kd, s_gbd = sem("s_kd"), sem("s_gbd")
        s_nf = sem("s_nf")
        s_sq2, s_ms2, s_rt2, s_t2, s_h2T = (
            sem(n) for n in ("s_sq2", "s_ms2", "s_rt2", "s_t2", "s_h2T"))
        s_qp = sem("s_qp")
        s_ps, s_psc = sem("s_ps"), sem("s_psc")
        s_tk, s_gm, s_gex, s_eid = sem("s_tk"), sem("s_gm"), sem("s_gex"), sem("s_eid")
        s_u = [sem(f"s_u{i}") for i in range(UV)]
        s_vv = [sem(f"s_vv{i}") for i in range(UV)]
        s_dot = sem("s_dot")
        s_gl = sem("s_gl")
        s_dg = sem("s_dg")
        s_ex = sem("s_ex")
        s_lone, s_lonev = sem("s_lone"), sem("s_lonev")
        s_fsq, s_frt, s_fin, s_out = (sem(n) for n in ("s_fsq", "s_frt", "s_fin", "s_out"))

        RPL = 2 * SPC
        gates_v = gates[:, :].rearrange("p (g t) -> p g t", g=GATES)
        block = top.enter_context(nc.Block())

        BODIES = CT // 2

        def behind(b, t, k):
            return (b, t - k) if t >= k else (b - 1, t - k + RPL)

        def flat(ap):
            return ap.rearrange("p a n -> p (a n)")

        @block.sync
        def _(sp):
            def load_weights(n0, i):
                for s in range(RING):
                    sp.wait_ge(s_wdone, n0 + s + 1 + RING * i)
                    sp.dma_start(ring[:, (n0 + s) % RING, :],
                                 W[bass.ds(n0 + s + RING * i, 1), :, :].rearrange("a p n -> (a p) n")
                                 ).then_inc(s_w[(n0 + s) % RING], 16)

            sp.dma_start(prm[:, :], par).then_inc(s_par, 16)
            for t in range(TT):
                sp.dma_start(xn[:, t, :], x[t * P:(t + 1) * P, :]).then_inc(s_x[t], 16)
            sp.dma_start(xs[0:META, TT, :], meta).then_inc(s_x[TT], 16)
            with sp.Fori(0, W_GATE // RING) as i:
                load_weights(0, i)
            with sp.Fori(0, CT // 2) as b:
                for cc in range(2):
                    sp.wait_ge(s_bu, SPC * (2 * b + cc) + 8)
                    sp.dma_start(bwt[:, cc, :, :, :].rearrange("p d r s -> p (d r s)"),
                                 bw[bass.ds(2 * b + cc, 1), :, :].rearrange("a p n -> (a p) n")).then_inc(s_bw[cc], 16)
                    sp.wait_ge(s_cp, 2 * (2 * b + cc) + 2)
                    sp.dma_start(cwt[:, cc, :, :, :].rearrange("p i r c -> p (i r c)"),
                                 cw[bass.ds(2 * b + cc, 1), :, :].rearrange("a p n -> (a p) n")).then_inc(s_cw[cc], 16)
                    load_weights(W_GATE + 4 * cc, 2 * b)
            with sp.Fori(0, (W_OUT - W_GLU) // RING) as i:
                load_weights(W_GLU, i)
            load_weights(W_OUT, 0)
            sp.wait_ge(s_mT, 2 + KT)
            sp.dma_start(gb[:, 0, :], gffn).then_inc(s_gbd, 16)
            sp.dma_start(keyt[:, :, :, :].rearrange("p h s n -> p (h s n)"), keys).then_inc(s_kd, 16)
            sp.dma_start(gb[:, 1, :], gfin).then_inc(s_kd, 16)
            with sp.Fori(0, (W_END - W_OUT) // RING - 1) as i:
                load_weights(W_OUT + RING, i)
            for t in range(TT):
                for c in range(2):
                    sp.wait_ge(s_fin, 2 * t + c + 1)
                    cols = slice(c * D // 2, (c + 1) * D // 2)
                    sp.dma_start(out[t * P:(t + 1) * P, cols], xn[:, t, cols]).then_inc(s_out, 16)
            sp.wait_ge(s_out, 2 * 16 * TT)

        @block.gpsimd
        def _(pool):
            pool.sem_inc(s_cp, 4)
            pool.sem_inc(s_os, 4)

            def out_matrices(b, cc):
                ct = 2 * b + cc
                pool.wait_ge(s_scur, 2 * ct + 2)
                pool.wait_ge(s_cw[cc], 16 * b + 16)
                cre, cim = cwt[:, cc, :, 0, :], cwt[:, cc, :, 1, :]

                def co(k):
                    return scur[:, cc, k, :].rearrange("p (i o) -> p i o", o=1).broadcast_to([P, SPC, 32])
                pool.wait_ge(s_cp, 2 * ct + 4)
                pool.tensor_tensor(cs[:, 0], cre, co(2), ALU.mult).then_inc(s_cpl, 1)
                pool.tensor_tensor(cs[:, 1], cim, co(3), ALU.mult).then_inc(s_cpl, 1)
                pool.tensor_tensor(cs[:, 2], cre, co(4), ALU.mult).then_inc(s_cpl, 1)
                pool.tensor_tensor(cs[:, 3], cim, co(2), ALU.mult).then_inc(s_cpl, 1)
                pool.wait_ge(s_cpl, 4 * ct + 4)
                pool.wait_ge(s_y, SPC * ct + 8)
                pool.tensor_tensor(cp[:, cc, 0], cs[:, 0], cs[:, 1], ALU.subtract).then_inc(s_cp, 1)
                pool.tensor_tensor(cp[:, cc, 1], cs[:, 2], cs[:, 3], ALU.subtract).then_inc(s_cp, 1)

            def turn_inputs(b, t):
                s, n = t % 2, RPL * b + t
                pool.wait_ge(s_ab, 2 * n + 6)
                pool.wait_ge(s_gst, 2 * n + 2)
                pool.tensor_tensor(gin[:, s, 0], pa[:, s, 0], pb[:, s, 0], ALU.add).then_inc(s_gin, 1)
                pool.tensor_tensor(gin[:, s, 1], pa[:, s, 1], pb[:, s, 1], ALU.subtract).then_inc(s_gin, 1)

            def turn_back(b, t):
                s, n, kept = t % 2, RPL * b + t, slice(0, SEQ) if t % 2 else slice(META, L)
                pool.wait_ge(s_gst, 2 * n + 6)
                pool.wait_ge(s_re, n + 1)
                pool.tensor_tensor(os_[:, s, :, 0:SEQ], trig[:, t % 4, 1:2, kept].broadcast_to([P, 2, SEQ]),
                                   gst[:, s, :, kept], ALU.mult).then_inc(s_os, 1)
                pool.wait_ge(s_os, n + 5)
                pool.wait_ge(s_oc, n + 5)
                pool.tensor_tensor(oc[:, s, 1, 0:SEQ], oc[:, s, 1, 0:SEQ], os_[:, s, 0, 0:SEQ], ALU.add).then_inc(s_im, 1)

            def scan_body(b, first=False):
                for t in range(RPL):
                    if t % SPC == 0:
                        out_matrices(b, t // SPC)
                    if t >= 1 or not first:
                        turn_inputs(*behind(b, t, 1))
                    if t >= 2 or not first:
                        turn_back(*behind(b, t, 2))

            scan_body(0, first=True)
            with pool.Fori(1, BODIES) as b:
                scan_body(b)
            turn_inputs(*behind(BODIES, 0, 1))
            turn_back(*behind(BODIES, 0, 2))
            turn_back(*behind(BODIES, 1, 2))
            for T in range(TT):
                with pool.Fori(0, PH // 2) as g:
                    for hh in range(2):
                        hd = T * PH + 2 * g + hh
                        pool.wait_ge(s_eid, hd + 1)
                        for j in range(TOPK):
                            m = hd * TOPK + j
                            s = j % UV
                            at = bass.IndirectOffsetOnAxis(ap=eid[:, hh, j:j + 1], axis=0)
                            pool.wait_ge(s_dot, m + 1)
                            pool.sem_inc(s_lone, 1)
                            pool.indirect_dma_start(uv[:, s, 0, :], None, u_tab, at).then_inc(s_u[s], 16)
                            pool.wait_ge(s_ex, m + 1)
                            pool.sem_inc(s_lone, 1)
                            pool.indirect_dma_start(uv[:, s, 1, :], None, v_tab, at).then_inc(s_vv[s], 16)

        @block.scalar
        def _(act):
            act.sem_inc(s_hT, 2)
            act.sem_inc(s_uk, 2)
            act.sem_inc(s_qT[0], 1)
            act.sem_inc(s_qT[1], 1)
            act.sem_inc(s_gs, 2)
            act.sem_inc(s_h2T, 2)
            act.sem_inc(s_qp, 2)
            act.sem_inc(s_psc, 2)
            act.wait_ge(s_f0, 1)
            nc.scalar.activation(disc[:, 6, :], disc[:, 4, :], ACT.Sin, scale=TWO_PI).then_inc(s_trig0, 1)
            nc.scalar.activation(disc[:, 7, :], disc[:, 4, :], ACT.Sin, scale=TWO_PI / 2).then_inc(s_trig0, 1)
            for t in range(TT + 1):
                rows = P if t < TT else META
                src = xn[:, t, :] if t < TT else xs[0:META, TT, :]
                act.wait_ge(s_x[t], 16)
                if t == 0:
                    act.wait_ge(s_ms, 1)
                if t > 0:
                    act.wait_ge(s_sq, t)
                nc.scalar.activation(hT[0:rows, 0:D], src, ACT.Square, accum_out=st[0:rows, t:t + 1]).then_inc(s_sq, 1)
            act.wait_ge(s_ms, 2)
            nc.scalar.activation(st[:, 4:7], st[:, 3 + 4:3 + 7], ACT.Sqrt).then_inc(s_sqr, 1)
            for k in range(KT):
                act.wait_ge(s_tr, k + 1)
                nc.scalar.activation(hTv[:, k, :], ps[:, k % 2, 0:L], ACT.Copy, scale=col("gmix", k, k + 1)).then_inc(s_hT, 1)
            for m in range(W_V):
                act.wait_ge(s_wdone, RING + m + 1)
                nc.scalar.activation(ukT[:, m, :], ps[:, m % 2, 0:L], ACT.Copy).then_inc(s_uk, 1)
            for t in range(TT):
                act.wait_ge(s_vp, t + 1)
                nc.scalar.activation(vr[:, t, :], ps[:, 2 + t, 0:KVH * HD], ACT.Copy).then_inc(s_ve, 1)
            act.wait_ge(s_wdone, RING + W_Q)
            nc.scalar.activation(vm[:, :], ps[0:META, 4, 0:KVH * HD], ACT.Copy).then_inc(s_ve, 1)

            def queries(h):
                act.wait_ge(s_wdone, RING + W_Q + h + 1)
                if h >= 2:
                    act.wait_ge(s_sc, 2 * (h - 1))
                nc.scalar.activation(qT[:, h % 2, :], ps[:, h % 2, 0:SEQ], ACT.Copy, scale=HD ** -0.5
                                     ).then_inc(s_qT[h % 2], 1)

            queries(0)
            for h in range(HEADS):
                for qb in range(TT):
                    a = 2 * h + qb
                    act.wait_ge(s_nm, a + 1)
                    if a >= 2:
                        act.wait_ge(s_pt, a - 1)
                    nc.scalar.activation(pr[:, qb, :], lg[:, qb, :], ACT.Exp, bias=sm[:, qb, 0:1],
                                         accum_out=sm[:, qb, 1:2]).then_inc(s_pe, 1)
                    if qb == 1 and h + 1 < HEADS:
                        queries(h + 1)

            def turns(b, t):
                n, cc = RPL * b + t, t // SPC
                if t % SPC == 0:
                    act.wait_ge(s_scur, 2 * (2 * b + cc) + 2)
                act.wait_ge(s_ang, n + 1)
                nc.scalar.activation(tb[:, t % 2, :], iota, ACT.Copy, scale=scur[:, cc, 0, t % SPC:t % SPC + 1]
                                     ).then_inc(s_tb, 1)

            def cos_sin(b, t):
                n = RPL * b + t
                act.wait_ge(s_ang, n + 3)
                act.wait_ge(s_oc, n + 1)
                act.wait_ge(s_os, n + 1)
                nc.scalar.activation(trig[:, t % 4, 1, :], ang[:, t % 2, 0, :], ACT.Sin, scale=-TWO_PI).then_inc(s_trg, 1)
                nc.scalar.activation(trig[:, t % 4, 0, :], ang[:, t % 2, 1, :], ACT.Sin, scale=-TWO_PI,
                                     bias=halfpi[:, :]).then_inc(s_trg, 1)

            def gate(b, t):
                q = t // 2
                g = SPC * b + q
                act.wait_ge(s_wdone, RING + W_GATE + 1 + g)
                nc.scalar.activation(flat(gates_v[:, bass.ds(g, 1), :]), ps[:, q % 2, 0:SEQ], ACT.Identity,
                                     bias=prm[:, bass.ds(COLS["bgate"][0] + g, 1)]).then_inc(s_gs, 1)

            def scan_body(b, first=False):
                for t in range(RPL):
                    turns(b, t)
                    if t >= 1 or not first:
                        cos_sin(*behind(b, t, 1))
                    if t % 2 and (t >= 2 or not first):
                        gate(*behind(b, t, 2))

            scan_body(0, first=True)
            with act.Fori(1, BODIES) as b:
                scan_body(b)
            cos_sin(*behind(BODIES, 0, 1))
            gate(*behind(BODIES, 1, 2))
            act.wait_ge(s_ye, 2 + CT)
            nc.scalar.activation(yT[:, :, :], yT[:, :, :], ACT.Gelu_apprx_tanh).then_inc(s_gel, 1)
            act.wait_ge(s_gs, 2 + GATES)
            nc.scalar.activation(gates[:, :], gates[:, :], ACT.Sigmoid).then_inc(s_sgg, 1)
            for m in range(CT):
                if m % 2 == 0:
                    act.wait_ge(s_glu, m // 2 + 1)
                else:
                    act.wait_ge(s_wdone, RING + W_GLU + m // 2 + 1)
                if m >= 2:
                    act.wait_ge(s_ya, m - 1)
                nc.scalar.activation(qT[:, m % 2, :], ps[:, m % 2, 0:SEQ], ACT.Sigmoid, bias=col("bglu", m, m + 1)
                                     ).then_inc(s_sig, 1)
            with act.Fori(0, 4) as c:
                for kk in range(4):
                    act.wait_ge(s_t2, 4 * c + kk + 1)
                    nc.scalar.activation(flat(h2T[:, bass.ds(4 * c + kk, 1), :]), ps[:, 4 + kk % 2, 0:SEQ], ACT.Copy,
                                         scale=prm[:, bass.ds(COLS["gffn"][0] + kk + 4 * c, 1)]).then_inc(s_h2T, 1)
            for T in range(TT):
                act.wait_ge(s_hs, 4 + TT * 4)
                act.wait_ge(s_ms2, 1)
                nc.scalar.activation(uv[:, 0, T, :], hs2[:, T, :], ACT.Square, accum_out=st[:, T:T + 1]).then_inc(s_sq2, 1)
            act.wait_ge(s_ms2, 2)
            nc.scalar.activation(st[:, 4:6], st[:, 7:9], ACT.Sqrt).then_inc(s_rt2, 1)

            def peer_query(q, pair):
                act.wait_ge(s_wdone, RING + W_PQ + 1 + q + 4 * pair)
                nc.scalar.activation(qp[:, q % 2, :], ps[:, 4 + q % 2, 0:SEQ], ACT.Copy).then_inc(s_qp, 1)

            def peer_scores(hh, pair):
                act.wait_ge(s_ps, hh + 2 * pair + 1)
                act.wait_ge(s_nf, 1)
                for T in range(TT):
                    ins = nc.scalar.activation(flat(sct[:, bass.ds(T * PH + hh + 2 * pair, 1), :]),
                                               ps[:, 6 + hh, T * 2 * NK:(T + 1) * 2 * NK], ACT.Copy, scale=st[:, 12 + T:13 + T])
                ins.then_inc(s_psc, 1)

            def gate_exp(hd, hh):
                act.wait_ge(s_gm, hd + 1)
                nc.scalar.activation(gw[:, hh, :], tv[:, 2, :], ACT.Exp, bias=gsum[:, 0:1],
                                     accum_out=gsum[:, 1:2]).then_inc(s_gex, 1)

            peer_query(0, 0)
            peer_query(1, 0)
            peer_scores(0, 0)
            gate_exp(0, 0)
            peer_query(2, 0)
            peer_query(3, 0)
            peer_scores(1, 0)

            def experts(T, g, last=False):
                for i in range(2 * TOPK):
                    hh, j = i // TOPK, i % TOPK
                    hd = T * PH + hh + 2 * g
                    act.wait_ge(s_dot, hd * TOPK + j + 1 + UV)
                    nc.scalar.activation(ga[:, hh, j:j + 1], av[:, hh, j:j + 1], ACT.Gelu_apprx_tanh).then_inc(s_gl, 1)
                    if j == 7 and not (last and T == TT - 1 and hh == 1):
                        gate_exp(hd + 1, 1 - hh)
                    if T == 0 and not last:
                        if i in (5, 9, 13, 17):
                            peer_query((i - 5) // 4, g + 1)
                        if i in (12, 20):
                            peer_scores((i - 12) // 8, g + 1)

            for T in range(TT):
                with act.Fori(0, PH // 2 - 1) as g:
                    experts(T, g)
                experts(T, PH // 2 - 1, last=True)
                act.wait_ge(s_ex, UV + (T + 1) * PH * TOPK)
                act.wait_ge(s_frt, 2 * T + 1)
                nc.scalar.activation(hs2[:, T, :], ps[:, 4 * T:4 * T + 4, :].rearrange("p b n -> p (b n)"), ACT.Square,
                                     accum_out=st[:, 10:11]).then_inc(s_fsq, 1)
                act.wait_ge(s_frt, 2 * T + 2)
                nc.scalar.activation(st[:, 12:13], st[:, 11:12], ACT.Sqrt).then_inc(s_fsq, 1)

        @block.vector
        def _(dve):
            dve.sem_inc(s_ab, 4)
            dve.sem_inc(s_gst, 4)
            dve.sem_inc(s_oc, 4)
            dve.sem_inc(s_ang, 2)
            dve.sem_inc(s_re, 2)
            dve.sem_inc(s_ye, 2)
            dve.sem_inc(s_pm, 2)
            dve.sem_inc(s_mT, 2)
            dve.sem_inc(s_hs, 4)
            dve.sem_inc(s_dot, UV)
            n_v = [0]

            def step(ins):
                n_v[0] += 1
                ins.then_inc(s_v, 1)
                dve.wait_ge(s_v, n_v[0])

            step(nc.vector.memset(halfpi[:, :], HALF_PI))
            nc.vector.memset(st[:, :], 1.0).then_inc(s_ms, 1)
            dve.wait_ge(s_par, 16)
            d = [disc[:, k, :] for k in range(24)]
            lre, lim, ldt = col("lam_re"), col("lam_im"), col("log_dt")
            step(nc.vector.tensor_scalar(d[0], ldt, 0.125, None, ALU.mult))
            step(nc.vector.tensor_scalar(d[1], d[0], float(1 / np.prod(np.arange(1.0, 11))), None, ALU.mult))
            for k in range(9, 0, -1):
                step(nc.vector.scalar_tensor_tensor(d[1], d[1], float(1 / np.prod(np.arange(1.0, k + 1))), d[0],
                                                    ALU.add, ALU.mult))
            step(nc.vector.tensor_scalar(d[1], d[1], 1.0, None, ALU.add))
            for _ in range(3):
                step(nc.vector.tensor_tensor(d[1], d[1], d[1], ALU.mult))
            step(nc.vector.tensor_tensor(d[2], lre, d[1], ALU.mult))
            step(nc.vector.tensor_scalar(d[2], d[2], -200.0, 1.0 / 128, ALU.max, ALU.mult))
            step(nc.vector.tensor_scalar(d[3], d[2], 1.0 / 720, None, ALU.mult))
            for k in range(5, 0, -1):
                step(nc.vector.scalar_tensor_tensor(d[3], d[3], float(1 / np.prod(np.arange(1.0, k + 1))), d[2],
                                                    ALU.add, ALU.mult))
            for _ in range(7):
                step(nc.vector.scalar_tensor_tensor(d[3], d[3], 2.0, d[3], ALU.add, ALU.mult))
            step(nc.vector.tensor_tensor(d[5], lim, d[1], ALU.mult))
            step(nc.vector.tensor_scalar(d[5], d[5], float(1 / (2 * np.pi)), None, ALU.mult))
            step(nc.vector.tensor_scalar(d[8], d[5], MAGIC, None, ALU.add))
            step(nc.vector.scalar_tensor_tensor(d[9], d[8], MAGIC, d[5], ALU.subtract, ALU.subtract))
            nc.vector.tensor_scalar(d[4], d[9], -1.0, None, ALU.mult).then_inc(s_f0, 1)
            step(nc.vector.tensor_scalar(d[10], d[3], 1.0, None, ALU.add))
            dve.wait_ge(s_trig0, 2)
            step(nc.vector.scalar_tensor_tensor(d[11], d[7], -2.0, d[7], ALU.mult, ALU.mult))
            step(nc.vector.tensor_scalar(d[12], d[11], 1.0, None, ALU.add))
            step(nc.vector.tensor_tensor(d[12], d[12], d[3], ALU.mult))
            step(nc.vector.tensor_tensor(d[12], d[12], d[11], ALU.add))
            step(nc.vector.tensor_tensor(d[13], d[6], d[10], ALU.mult))
            step(nc.vector.tensor_tensor(d[14], lre, lre, ALU.mult))
            step(nc.vector.tensor_tensor(d[15], lim, lim, ALU.mult))
            step(nc.vector.tensor_tensor(d[14], d[14], d[15], ALU.add))
            step(nc.vector.reciprocal(d[14], d[14]))
            step(nc.vector.tensor_tensor(d[16], d[12], lre, ALU.mult))
            step(nc.vector.tensor_tensor(d[17], d[13], lim, ALU.mult))
            step(nc.vector.tensor_tensor(d[16], d[16], d[17], ALU.add))
            step(nc.vector.tensor_tensor(d[16], d[16], d[14], ALU.mult))
            step(nc.vector.tensor_tensor(d[18], d[13], lre, ALU.mult))
            step(nc.vector.tensor_tensor(d[19], d[12], lim, ALU.mult))
            step(nc.vector.tensor_tensor(d[18], d[18], d[19], ALU.subtract))
            step(nc.vector.tensor_tensor(d[18], d[18], d[14], ALU.mult))
            step(nc.vector.tensor_scalar(d[19], d[18], -1.0, None, ALU.mult))
            for k, a in enumerate((4, 10, 16, 18, 19)):
                nc.vector.tensor_copy(scal[:, :, k, :], d[a].rearrange("p (c i) -> p c i", i=SPC))
            for i in range(SPC):
                ins = nc.vector.tensor_copy(scal[:, :, 5, i], col("dskip"))
            step(ins)

            def rstd(dst, ss, v, root):
                step(nc.vector.reciprocal(dst, root))
                step(nc.vector.tensor_tensor(ss, dst, dst, ALU.mult))
                step(nc.vector.tensor_tensor(ss, ss, v, ALU.mult))
                step(nc.vector.tensor_scalar(ss, ss, -0.5, 1.5, ALU.mult, ALU.add))
                step(nc.vector.tensor_tensor(dst, dst, ss, ALU.mult))

            dve.wait_ge(s_sq, TT + 1)
            nc.vector.tensor_scalar(st[:, 7:10], st[:, 0:3], 1.0 / D, EPS, ALU.mult, ALU.add).then_inc(s_ms, 1)
            dve.wait_ge(s_ms, 2)
            dve.wait_ge(s_sqr, 1)
            rstd(st[:, 12:15], st[:, 0:3], st[:, 7:10], st[:, 4:7])
            for t in range(TT):
                nc.vector.tensor_scalar(xs[:, t, :], xn[:, t, :], st[:, 12 + t:13 + t], None, ALU.mult).then_inc(s_xs, 1)
            nc.vector.tensor_scalar(xs[0:META, TT, :], xs[0:META, TT, :], st[0:META, 14:15], None, ALU.mult
                                    ).then_inc(s_xs, 1)

            def softmax_front(h, qb):
                a = 2 * h + qb
                dve.wait_ge(s_sc, a + 1)
                nc.vector.scalar_tensor_tensor(lg[:, qb, 0:L], alibi[:, qb, :], float(2.0 ** (-8.0 * (h + 1) / HEADS)),
                                               ps[:, 6 + qb, 0:L], ALU.mult, ALU.add).then_inc(s_lg, 1)
                nc.vector.tensor_copy(lg[:, qb, L:L + 1], col("sink", h, h + 1)).then_inc(s_lg, 1)
                dve.wait_ge(s_lg, 2 * a + 2)
                nc.vector.tensor_reduce(sm[:, qb, 0:1], lg[:, qb, :], AX_X, ALU.max, negate=True).then_inc(s_nm, 1)

            def softmax_back(h, qb):
                a = 2 * h + qb
                dve.wait_ge(s_pe, a + 1)
                nc.vector.reciprocal(sm[:, qb, 2:3], sm[:, qb, 1:2]).then_inc(s_al, 1)
                dve.wait_ge(s_al, a + 1)
                nc.vector.tensor_scalar(pr[:, qb, 0:L], pr[:, qb, 0:L], sm[:, qb, 2:3], None, ALU.mult).then_inc(s_pn, 1)

            def weights_T(h, qb):
                a = 2 * h + qb
                dve.wait_ge(s_pt, a + 1)
                nc.vector.tensor_copy(pT[0:META, qb, 0:P], ps[0:META, 2 + qb, 0:P]).then_inc(s_pT, 1)
                nc.vector.tensor_copy(pT[:, qb, P:3 * P], ps[:, 2 + qb, P:3 * P]).then_inc(s_pT, 1)

            def values(h, qb):
                a = 2 * h + qb
                dve.wait_ge(s_av, a + 1)
                nc.vector.tensor_copy(ybT[:, h, qb * P:(qb + 1) * P], ps[:, 4 + qb, 0:P]).then_inc(s_yb, 1)

            for h in range(HEADS):
                softmax_front(h, 0)
                softmax_back(h, 0)
                softmax_front(h, 1)
                weights_T(h, 0)
                softmax_back(h, 1)
                values(h, 0)
                weights_T(h, 1)
                values(h, 1)

            dve.wait_ge(s_uk, 2 + W_V)

            def scalars(b, cc):
                ct = 2 * b + cc
                nc.vector.tensor_copy(scur[:, cc].rearrange("p k i -> p (k i)"),
                                      scal[:, bass.ds(ct, 1), :, :].rearrange("p a k i -> p (a k i)")).then_inc(s_scur, 1)
                nc.vector.tensor_copy(ucur[:, cc, :], flat(ukT[:, bass.ds(ct, 1), :])).then_inc(s_scur, 1)
                dve.wait_ge(s_scur, 2 * ct + 2)

            def angles(b, t):
                s, n = t % 2, RPL * b + t
                nc.vector.tensor_scalar(tb[:, 2, :], iota, scur[:, t // SPC, 0, t % SPC:t % SPC + 1], MAGIC,
                                        ALU.mult, ALU.add).then_inc(s_vl, 1)
                dve.wait_ge(s_vl, 2 * n + 1)
                dve.wait_ge(s_tb, n + 1)
                nc.vector.scalar_tensor_tensor(ang[:, s, 0, :], tb[:, 2, :], MAGIC, tb[:, s, :],
                                               ALU.subtract, ALU.subtract).then_inc(s_vl, 1)
                dve.wait_ge(s_vl, 2 * n + 2)
                nc.vector.scalar_tensor_tensor(ang[:, s, 1, :], ang[:, s, 0, :], -1.0, ang[:, s, 0, :],
                                               ALU.mult, ALU.max).then_inc(s_ang, 1)

            def input_products(b, t):
                s, n = t % 2, RPL * b + t
                dve.wait_ge(s_trg, 2 * n + 2)
                dve.wait_ge(s_bu, n + 17)
                bu = ps[:, 2 + 2 * s:4 + 2 * s, 0:L]
                cos = trig[:, t % 4, 0:1, :].broadcast_to([P, 2, L])
                nc.vector.tensor_tensor(pa[:, s], bu, cos, ALU.mult).then_inc(s_ab, 1)
                sin = trig[:, t % 4, 1:2, :].broadcast_to([P, 2, L])
                nc.vector.tensor_tensor(pb[:, s], ps[:, 3 + 2 * s:1 + 2 * s:-1, 0:L], sin, ALU.mult).then_inc(s_ab, 1)

            def scans(b, t):
                s, n = t % 2, RPL * b + t
                dve.wait_ge(s_gin, 2 * n + 2)
                dve.wait_ge(s_os, n + 3)
                r = scur[:, t // SPC, 1, t % SPC:t % SPC + 1].broadcast_to([P, L])
                for k in range(2):
                    nc.vector.tensor_tensor_scan(gst[:, s, k, :], r, gin[:, s, k, :], 0.0, ALU.mult, ALU.add
                                                 ).then_inc(s_gst, 1)

            def cos_products(b, t):
                s, n, kept = t % 2, RPL * b + t, slice(0, SEQ) if t % 2 else slice(META, L)
                dve.wait_ge(s_gst, 2 * n + 6)
                dve.wait_ge(s_y, n + 15)
                nc.vector.tensor_tensor(oc[:, s, :, 0:SEQ], trig[:, t % 4, 0:1, kept].broadcast_to([P, 2, SEQ]),
                                        gst[:, s, :, kept], ALU.mult).then_inc(s_oc, 1)

            def real_parts(b, t):
                s, n = t % 2, RPL * b + t
                dve.wait_ge(s_oc, n + 5)
                dve.wait_ge(s_os, n + 5)
                nc.vector.tensor_tensor(oc[:, s, 0, 0:SEQ], oc[:, s, 0, 0:SEQ], os_[:, s, 1, 0:SEQ], ALU.subtract
                                        ).then_inc(s_re, 1)

            def take_y(b, cc):
                ct = 2 * b + cc
                dve.wait_ge(s_y, SPC * ct + SPC + 16)
                nc.vector.scalar_tensor_tensor(flat(yT[:, bass.ds(ct, 1), :]), ucur[:, cc, META:L],
                                               scur[:, cc, 5, 0:1], ps[:, 6 + cc, 0:SEQ], ALU.mult, ALU.add
                                               ).then_inc(s_ye, 1)

            def scan_body(b, first=False):
                for t in range(RPL):
                    if t % SPC == 0:
                        scalars(b, t // SPC)
                    angles(b, t)
                    if t >= 1 or not first:
                        input_products(*behind(b, t, 1))
                    if t >= 2 or not first:
                        scans(*behind(b, t, 2))
                    if t >= 3 or not first:
                        real_parts(*behind(b, t, 3))
                    if t >= 2 or not first:
                        cos_products(*behind(b, t, 2))
                    if t == SPC + 4:
                        take_y(b, 0)
                    if t == 4 and not first:
                        take_y(b - 1, 1)

            scan_body(0, first=True)
            with dve.Fori(1, BODIES) as b:
                scan_body(b)
            input_products(*behind(BODIES, 0, 1))
            for t in range(2):
                scans(*behind(BODIES, t, 2))
                real_parts(*behind(BODIES, t, 3))
                cos_products(*behind(BODIES, t, 2))
            real_parts(*behind(BODIES, 2, 3))
            take_y(BODIES - 1, 1)

            dve.wait_ge(s_gel, 1)
            for m in range(CT):
                dve.wait_ge(s_sig, m + 1)
                nc.vector.tensor_tensor(yaT[:, m, :], yT[:, m, :], qT[:, m % 2, :], ALU.mult).then_inc(s_ya, 1)
            dve.wait_ge(s_sgg, 1)
            with dve.Fori(0, KT // 4) as i:
                for q in range(4):
                    dve.wait_ge(s_wdone, RING + W_PROJ + 1 + q + 4 * i)
                    dve.wait_ge(s_mT, 1 + q + 4 * i)
                    nc.vector.tensor_tensor(pa[:, q % 2, :, 0:SEQ], gt[:, :, bass.ds(q + 4 * i, 1), :].rearrange("p b a t -> p b (a t)"),
                                            ps[:, q % 2, :].rearrange("p (b t) -> p b t", b=2), ALU.mult).then_inc(s_pm, 1)
                    dve.wait_ge(s_pm, 3 + q + 4 * i)
                    nc.vector.tensor_tensor(flat(mT[:, bass.ds(q + 4 * i, 1), :]), pa[:, q % 2, 0, 0:SEQ],
                                            pa[:, q % 2, 1, 0:SEQ], ALU.add).then_inc(s_mT, 1)
            with dve.Fori(0, 2) as i:
                for q in range(2):
                    for T in range(TT):
                        dve.wait_ge(s_wdone, RING + W_OUT + 4 * q + 4 + 8 * i)
                        nc.vector.tensor_tensor(hs2[:, T, bass.ds(512 * q + 1024 * i, 512)], ps[:, 2 * q + T, :],
                                                xn[:, T, bass.ds(512 * q + 1024 * i, 512)], ALU.add).then_inc(s_hs, 1)
            nc.vector.memset(st[:, 0:2], 1.0).then_inc(s_ms2, 1)
            dve.wait_ge(s_sq2, TT)
            nc.vector.tensor_scalar(st[:, 7:9], st[:, 0:2], 1.0 / D, EPS, ALU.mult, ALU.add).then_inc(s_ms2, 1)
            dve.wait_ge(s_rt2, 1)
            dve.wait_ge(s_ms2, 2)
            rstd(st[:, 12:14], st[:, 0:2], st[:, 7:9], st[:, 4:6])
            dve.sem_inc(s_nf, 1)
            dve.wait_ge(s_gbd, 16)
            for T in range(TT):
                nc.vector.scalar_tensor_tensor(xn[:, T, :], hs2[:, T, :], st[:, 12 + T:13 + T], gb[:, 0, :],
                                               ALU.mult, ALU.mult).then_inc(s_ms2, 1)
            dve.wait_ge(s_ms2, 2 + TT)

            def top16(vals, idxs, src, spare):
                yield nc.vector.max(vals[:, 0:8], src)
                yield nc.vector.max_index(idxs[:, 0:8], vals[:, 0:8], src)
                yield nc.vector.match_replace(spare, vals[:, 0:8], src, NEG)
                yield nc.vector.max(vals[:, 8:16], spare)
                yield nc.vector.max_index(idxs[:, 8:16], vals[:, 8:16], spare)

            TK = 31

            def select(hd, hh):
                k = [0]

                def tl(ins):
                    k[0] += 1
                    ins.then_inc(s_tk, 1)
                    dve.wait_ge(s_tk, hd * TK + k[0])
                    dve.sem_inc(s_lonev, 1)

                yield tl(nc.vector.tensor_copy(ks[:, :], flat(sct[:, bass.ds(hd, 1), :])))
                for s in range(2):
                    for ins in top16(tv[:, s, :], ti[:, s, :], ks[:, s * NK:(s + 1) * NK], kr[:, s * NK:(s + 1) * NK]):
                        yield tl(ins)
                    yield tl(nc.vector.tensor_copy(tif[:, s, :], ti[:, s, :]))

                def rows(ap):
                    return ap.rearrange("p (a o) -> p a o", o=1).broadcast_to([P, TOPK, TOPK])

                def cols_(ap):
                    return ap.rearrange("p (o a) -> p o a", o=1).broadcast_to([P, TOPK, TOPK])
                yield tl(nc.vector.tensor_tensor(cand[:, :, :], rows(tv[:, 0, :]), cols_(tv[:, 1, :]), ALU.add))
                cf, of = cand[:, :, :].rearrange("p a b -> p (a b)"), oh[:, :, :].rearrange("p a b -> p (a b)")
                for ins in top16(tv[:, 2, :], ti[:, 2, :], cf, of):
                    yield tl(ins)
                nc.vector.tensor_scalar(gsum[:, 0:1], tv[:, 2, 0:1], -1.0, None, ALU.mult).then_inc(s_gm, 1)
                yield tl(nc.vector.tensor_scalar(tq[:, 0, :], ti[:, 2, :], 4, None, ALU.logical_shift_right))
                yield tl(nc.vector.tensor_scalar(tq[:, 1, :], ti[:, 2, :], TOPK - 1, None, ALU.bitwise_and))
                for s in range(2):
                    yield tl(nc.vector.tensor_copy(tif[:, 2 + s, :], tq[:, s, :]))
                    yield tl(nc.vector.tensor_tensor(oh[:, :, :], rows(tif[:, 2 + s, :]), cols_(col("iota16")), ALU.is_equal))
                    yield tl(nc.vector.tensor_tensor(oh[:, :, :], oh[:, :, :], cols_(tif[:, s, :]), ALU.mult))
                    yield tl(nc.vector.tensor_reduce(tif[:, 2 + s, :], oh[:, :, :], AX_X, ALU.add))
                nc.vector.scalar_tensor_tensor(eid[:, hh, :], tif[:, 2, :], float(NK), tif[:, 3, :], ALU.mult, ALU.add
                                               ).then_inc(s_eid, 1)
                dve.wait_ge(s_gex, hd + 1)
                yield tl(nc.vector.reciprocal(gsum[:, 2:3], gsum[:, 1:2]))
                yield tl(nc.vector.tensor_scalar(gw[:, hh, :], gw[:, hh, :], gsum[:, 2:3], None, ALU.mult))
                assert k[0] == TK, k[0]

            def experts(T, g, last=False):
                for hh in range(2):
                    hd = T * PH + hh + 2 * g
                    if last and hh == 1:
                        picks = select(hd + 1, 0) if T < TT - 1 else iter(())
                    else:
                        picks = select(hd + 1, 1 - hh)
                        if T == 0:
                            dve.wait_ge(s_psc, 4 + hh + 2 * g)
                    for j in range(TOPK):
                        m = hd * TOPK + j
                        dve.wait_ge(s_u[j % UV], 16 * (hd * (TOPK // UV) + j // UV + 1))
                        nc.vector.tensor_tensor_reduce(uv[:, j % UV, 0, :], uv[:, j % UV, 0, :], xn[:, T, :], 1.0, 0.0,
                                                       ALU.mult, ALU.add, av[:, hh, j:j + 1]).then_inc(s_dot, 1)
                        for _ in range(3):
                            next(picks, None)
                        dve.wait_ge(s_gl, m + 1)
                        dve.wait_ge(s_ex, m + 1 + (UV - 2))
                        nc.vector.tensor_scalar(dg[:, j % 2, :], ident, ga[:, hh, j:j + 1], gw[:, hh, j:j + 1],
                                                ALU.mult, ALU.mult).then_inc(s_dg, 1)

            dve.wait_ge(s_psc, 3)
            for _ in select(0, 0):
                pass
            for T in range(TT):
                with dve.Fori(0, PH // 2 - 1) as g:
                    experts(T, g)
                experts(T, PH // 2 - 1, last=True)
                nc.vector.memset(st[:, 10:11], 0.0).then_inc(s_frt, 1)
                dve.wait_ge(s_fsq, 2 * T + 1)
                nc.vector.tensor_scalar(st[:, 11:12], st[:, 10:11], 1.0 / D, EPS, ALU.mult, ALU.add).then_inc(s_frt, 1)
                dve.wait_ge(s_frt, 2 * T + 2)
                dve.wait_ge(s_fsq, 2 * T + 2)
                rstd(st[:, 13:14], st[:, 14:15], st[:, 11:12], st[:, 12:13])
                dve.wait_ge(s_kd, 32)
                for c in range(2):
                    cols = slice(c * D // 2, (c + 1) * D // 2)
                    nc.vector.scalar_tensor_tensor(xn[:, T, cols], ps[:, 4 * T + 2 * c:4 * T + 2 * c + 2, :].rearrange("p b n -> p (b n)"),
                                                   st[:, 13:14], gb[:, 1, cols], ALU.mult, ALU.mult).then_inc(s_fin, 1)

        @block.tensor
        def _(pe):
            pe.sem_inc(s_wdone, RING)
            pe.sem_inc(s_bu, 16)
            pe.sem_inc(s_y, 16)
            pe.sem_inc(s_ex, UV)

            def weights_in(n0, i=0):
                pe.wait_ge(s_w[n0 % RING], 16 * (n0 // RING + 1) + 16 * i)

            def product(dst, n0, rhs, kts=KT, block0=0, m=KT, k0=0):
                w = wtile(n0, m, P)
                for k in range(kts):
                    ins = nc.tensor.matmul(dst, w[:, block0 + k, :], rhs(k0 + k), start=(k == 0), stop=(k == kts - 1))
                return ins

            pe.wait_ge(s_par, 16)
            pe.wait_ge(s_xs, TT + 1)
            for k in range(KT):
                pe.wait_ge(s_hT, k + 1)
                c = slice(k * P, (k + 1) * P)
                nc.tensor.transpose(ps[:, k % 2, 0:META], xs[0:META, TT, c], ident[0:META, 0:META])
                for t in range(TT):
                    ins = nc.tensor.transpose(ps[:, k % 2, META + t * P:META + (t + 1) * P], xs[:, t, c], ident)
                ins.then_inc(s_tr, 1)
            pe.wait_ge(s_hT, 2 + KT)
            for m in range(W_V):
                weights_in(m)
                pe.wait_ge(s_uk, m + 1)
                product(ps[:, m % 2, 0:L], m, lambda k: hTv[:, k, :]).then_inc(s_wdone, 1)
            weights_in(W_V)
            weights_in(W_V + 1)
            for t in range(TT + 1):
                rows, c = (P, slice(META + t * P, META + (t + 1) * P)) if t < TT else (META, slice(0, META))
                for k in range(KT):
                    w = wtile(W_V + k // 8, 8, KVH * HD)
                    ins = nc.tensor.matmul(ps[0:rows, 2 + t, 0:KVH * HD], hTv[:, k, c], w[:, k % 8, :],
                                           start=(k == 0), stop=(k == KT - 1))
                ins.then_inc(*((s_vp, 1) if t < TT else (s_wdone, 2)))

            def queries(h, part):
                n = W_Q + h
                if part == 0:
                    weights_in(n)
                    if h >= 2:
                        pe.wait_ge(s_qT[h % 2], h // 2 + 1)
                w = wtile(n, KT, P)
                for k in range(8 * part, 8 * part + 8):
                    ins = nc.tensor.matmul(ps[:, h % 2, 0:SEQ], w[:, k, :], hTv[:, k, META:L],
                                           start=(k == 0), stop=(k == KT - 1))
                if part:
                    ins.then_inc(s_wdone, 1)

            def scores(h, qb):
                a = 2 * h + qb
                if qb == 0:
                    pe.wait_ge(s_qT[h % 2], h // 2 + 2)
                if a >= 2:
                    pe.wait_ge(s_lg, 2 * (a - 2) + 1)
                nc.tensor.matmul(ps[:, 6 + qb, 0:L], qT[:, h % 2, qb * P:(qb + 1) * P], ukT[:, CT + h // 4, :],
                                 start=True, stop=True).then_inc(s_sc, 1)

            def transposes(h, qb):
                a = 2 * h + qb
                pe.wait_ge(s_pn, a + 1)
                if a >= 2:
                    pe.wait_ge(s_pT, 2 * (a - 1))
                if a == 0:
                    pe.wait_ge(s_ve, TT + 1)
                b0 = ps[:, 2 + qb, :]
                nc.tensor.transpose(b0[0:META, 0:P], pr[:, qb, 0:META], ident)
                for t in range(TT):
                    ins = nc.tensor.transpose(b0[:, (t + 1) * P:(t + 2) * P], pr[:, qb, META + t * P:META + (t + 1) * P], ident)
                ins.then_inc(s_pt, 1)

            def values(h, qb):
                a = 2 * h + qb
                kv = slice(h // 4 * HD, (h // 4 + 1) * HD)
                pe.wait_ge(s_pT, 2 * a + 2)
                if a >= 2:
                    pe.wait_ge(s_yb, a - 1)
                o = ps[:, 4 + qb, 0:P]
                nc.tensor.matmul(o, vr[:, 0, kv], pT[:, qb, P:2 * P], start=True, stop=False)
                nc.tensor.matmul(o, vr[:, 1, kv], pT[:, qb, 2 * P:3 * P], start=False, stop=False)
                nc.tensor.matmul(o, vm[:, kv], pT[0:META, qb, 0:P], start=False, stop=True).then_inc(s_av, 1)

            pe.wait_ge(s_uk, 2 + W_V)
            queries(0, 0)
            queries(0, 1)
            for h in range(HEADS):
                scores(h, 0)
                if h + 1 < HEADS:
                    queries(h + 1, 0)
                transposes(h, 0)
                scores(h, 1)
                if h + 1 < HEADS:
                    queries(h + 1, 1)
                values(h, 0)
                transposes(h, 1)
                values(h, 1)

            pe.wait_ge(s_yb, 2 * HEADS)
            pe.wait_ge(s_pT, 4 * HEADS)
            def state_inputs(b, t):
                s, n, cc, j, way = t % 2, RPL * b + t, t // SPC, t % SPC // 2, t % 2
                if t % SPC == 0:
                    pe.wait_ge(s_bw[cc], 16 * b + 16)
                    pe.wait_ge(s_scur, 2 * (2 * b + cc) + 2)
                pe.wait_ge(s_ab, 2 * n + 2)
                rows = slice(32 * j, 32 * j + 32)
                u = ucur[rows, cc, :]
                if way:
                    u = u[:, L - 1::-1]
                for r in range(2):
                    ins = nc.tensor.matmul(ps[:, 2 + 2 * s + r, 0:L], bwt[rows, cc, way, r, :], u, start=True, stop=True)
                ins.then_inc(s_bu, 1)

            def half_gate(b, t):
                q = t // 2
                if t % 2 == 0:
                    weights_in(W_GATE + q, 2 * b)
                    pe.wait_ge(s_gs, SPC * b + q + 1)
                w = wtile(W_GATE + q, KT, P)
                for k in range(8 * (t % 2), 8 * (t % 2) + 8):
                    ins = nc.tensor.matmul(ps[:, q % 2, 0:SEQ], w[:, k, :], hTv[:, k, META:L],
                                           start=(k == 0), stop=(k == KT - 1))
                if t % 2:
                    ins.then_inc(s_wdone, 1)

            def state_outputs(b, t):
                s, n, cc, i = t % 2, RPL * b + t, t // SPC, t % SPC
                j, way = i // 2, i % 2
                pe.wait_ge(s_re, n + 3)
                pe.wait_ge(s_im, n + 1)
                if i == 0:
                    pe.wait_ge(s_cp, 2 * (2 * b + cc) + 6)
                    pe.wait_ge(s_ye, 2 * b + cc + 1)
                for k in range(2):
                    rhs = oc[:, s, k, SEQ - 1::-1] if way else oc[:, s, k, 0:SEQ]
                    ins = nc.tensor.matmul(ps[32 * j:32 * j + 32, 6 + cc, 0:SEQ], cp[:, cc, k, i, :], rhs,
                                           start=(way == 0 and k == 0), stop=(way == 1 and k == 1))
                ins.then_inc(s_y, 1)

            def scan_body(b, first=False):
                for t in range(RPL):
                    state_inputs(b, t)
                    half_gate(b, t)
                    if t >= 3 or not first:
                        state_outputs(*behind(b, t, 3))

            scan_body(0, first=True)
            with pe.Fori(1, BODIES) as b:
                scan_body(b)
            for t in range(3):
                state_outputs(*behind(BODIES, t, 3))

            pe.wait_ge(s_gel, 1)
            pe.wait_ge(s_gs, 2 + GATES)
            for m in range(CT):
                if m % 2 == 0:
                    weights_in(W_GLU + m // 2)
                if m >= 2:
                    pe.wait_ge(s_sig, m - 1)
                product(ps[:, m % 2, 0:SEQ], W_GLU + m // 2, lambda k: yT[:, k, :], kts=CT, block0=CT * (m % 2)
                        ).then_inc(*((s_glu, 1) if m % 2 == 0 else (s_wdone, 1)))
            pe.wait_ge(s_ya, CT)
            with pe.Fori(0, KT // 4) as i:
                for q in range(4):
                    weights_in(W_PROJ + q, i)
                    pe.wait_ge(s_pm, 1 + q + 4 * i)
                    product(ps[:, q % 2, 0:SEQ], W_PROJ + q, lambda k: yaT[:, k, :], kts=CT)
                    product(ps[:, q % 2, SEQ:2 * SEQ], W_PROJ + q, lambda k: ybT[:, k, :], kts=HEADS, block0=CT
                            ).then_inc(s_wdone, 1)
            pe.wait_ge(s_mT, KT + 2)

            def row_transposes(c):
                pe.wait_ge(s_hs, 4 + 2 * (c + 1))
                for k in range(4 * c, 4 * c + 4):
                    pe.wait_ge(s_h2T, k + 1)
                    for T in range(TT):
                        ins = nc.tensor.transpose(ps[:, 4 + k % 2, T * P:(T + 1) * P], hs2[:, T, k * P:(k + 1) * P], ident)
                    ins.then_inc(s_t2, 1)

            for c in range(4):
                pe.wait_ge(s_hs, 2 * c + 2)
                for g in range(4):
                    weights_in(W_OUT + 4 * c + g)
                    w = wtile(W_OUT + 4 * c + g, 4, 512)
                    for k in range(4 * g, 4 * g + 4):
                        for T in range(TT):
                            ins = nc.tensor.matmul(ps[:, 2 * (c % 2) + T, :], mT[:, k, T * P:(T + 1) * P], w[:, k % 4, :],
                                                   start=(k == 0), stop=(k == KT - 1))
                    ins.then_inc(s_wdone, 1)
                    if c and g == 0:
                        row_transposes(c - 1)
            row_transposes(3)
            pe.wait_ge(s_h2T, 2 + KT)
            pe.wait_ge(s_kd, 32)

            def peer_query(q, pair, part):
                if part == 0:
                    weights_in(W_PQ + q, pair)
                    pe.wait_ge(s_qp, 1 + q + 4 * pair)
                w = wtile(W_PQ + q, KT, P)
                for k in range(8 * part, 8 * part + 8):
                    ins = nc.tensor.matmul(ps[:, 4 + q % 2, 0:SEQ], w[:, k, :], h2T[:, k, :], start=(k == 0), stop=(k == KT - 1))
                if part:
                    ins.then_inc(s_wdone, 1)

            def peer_scores(q, pair):
                hh, half = q // 2, q % 2
                pe.wait_ge(s_qp, 3 + q + 4 * pair)
                if half == 0:
                    pe.wait_ge(s_psc, 1 + hh + 2 * pair)
                for T in range(TT):
                    ins = nc.tensor.matmul(ps[:, 6 + hh, T * 2 * NK + half * NK:T * 2 * NK + (half + 1) * NK],
                                           qp[:, half, T * P:(T + 1) * P],
                                           keyt[:, bass.ds(2 * pair + hh, 1), half, :].rearrange("p a n -> p (a n)"),
                                           start=True, stop=True)
                if half:
                    ins.then_inc(s_ps, 1)

            for q in range(4):
                peer_query(q, 0, 0)
                peer_query(q, 0, 1)
                if q == 1:
                    peer_scores(0, 0)
                    peer_scores(1, 0)
            peer_scores(2, 0)
            peer_scores(3, 0)

            def experts(T, g, last=False):
                for i in range(2 * TOPK):
                    hh, j = i // TOPK, i % TOPK
                    hd = T * PH + hh + 2 * g
                    pe.wait_ge(s_dg, hd * TOPK + j + 1)
                    pe.wait_ge(s_vv[j % UV], 16 * (hd * (TOPK // UV) + j // UV + 1))
                    for n in range(4):
                        ins = nc.tensor.matmul(ps[:, 4 * T + n, :], dg[:, j % 2, :], uv[:, j % UV, 1, n * 512:(n + 1) * 512],
                                               start=False, stop=last and i == 2 * TOPK - 1, skip_group_check=True)
                    ins.then_inc(s_ex, 1)
                    if T == 0 and not last:
                        if i % 2 and i < 16:
                            peer_query(i // 4, g + 1, i // 2 % 2)
                        if i in (6, 10, 14, 18):
                            peer_scores((i - 6) // 4, g + 1)

            for T in range(TT):
                if T == 1:
                    pe.wait_ge(s_psc, 2 + PH)
                for n in range(4):
                    nc.tensor.matmul(ps[:, 4 * T + n, :], ident, hs2[:, T, n * 512:(n + 1) * 512], start=True, stop=False,
                                     skip_group_check=True)
                with pe.Fori(0, PH // 2 - 1) as g:
                    experts(T, g)
                experts(T, PH // 2 - 1, last=True)


def lay_out(a):
    f = lambda n: np.asarray(a[n], np.float32) if np.asarray(a[n]).dtype != np.float32 else np.asarray(a[n])
    w_in = f("w_in")[0]

    def tiles(w):
        k, n = w.shape
        return w.reshape(k // P, P, n // P, P).transpose(2, 1, 0, 3).reshape(n // P, P, k)

    def rows(w, c):
        k, n = w.shape
        m = D // c
        return w.reshape(k // P // m, m, P, n // c, c).transpose(3, 0, 2, 1, 4).reshape(-1, P, D)

    q0, k0, v0, g0 = SSM_W, SSM_W + HEADS * HD, SSM_W + HEADS * HD + KVH * HD, SSM_W + HEADS * HD + 2 * KVH * HD
    glu = tiles(f("ssm_w_glu")[0]).reshape(CT // 2, 2, P, SSM_W).transpose(0, 2, 1, 3).reshape(CT // 2, P, D)
    proj = np.concatenate([tiles(f("w_proj_ssm")[0]), tiles(f("w_proj_attn")[0])], axis=2)
    W = np.concatenate([tiles(w_in[:, 0:q0]), tiles(w_in[:, k0:v0]), rows(w_in[:, v0:g0], KVH * HD),
                        tiles(w_in[:, q0:k0]), tiles(w_in[:, g0:]), glu, proj, rows(f("w_out")[0], 512),
                        tiles(f("peer_w_q")[0])])
    assert W.shape == (W_END, P, D), W.shape
    keys = np.stack([f("peer_k1")[0], f("peer_k2")[0]]).transpose(3, 1, 0, 2).reshape(P, PH * 2 * NK)

    def states(v):
        return v.reshape(2, CT, SPC // 2, 2, ST).transpose(3, 4, 1, 2, 0).reshape(P, NST)

    def column(v, n):
        return v.reshape(n, P).T

    t = np.arange(SEQ)
    dist = np.abs(t[:, None] - t[None, :]).astype(np.float32)
    bias = np.where(dist <= WINDOW, -dist, np.float32(-1e30)).astype(np.float32)
    alibi = np.concatenate([np.zeros((SEQ, META), np.float32), bias], 1).reshape(TT, P, L).transpose(1, 0, 2).reshape(P, TT * L)
    ldt = np.broadcast_to(f("ssm_log_dt")[0][:, :, None], (2, GROUPS, ST))
    par = np.concatenate([
        column(f("norm_mix")[0], KT), column(f("b_gate")[0], GATES), column(f("ssm_d")[0], CT),
        column(f("ssm_b_glu")[0], CT), np.broadcast_to(f("attn_sink")[0], (P, HEADS)),
        states(f("ssm_lam_re")[0]), states(f("ssm_lam_im")[0]), states(ldt),
        np.broadcast_to(np.arange(L, dtype=np.float32), (P, L)), np.eye(P, dtype=np.float32), alibi,
        np.broadcast_to(np.arange(TOPK, dtype=np.float32), (P, TOPK)), column(f("norm_ffn")[0], KT)], axis=1)
    bw = np.zeros((CT, SPC // 2, 2, GC, 2, 2, 2, ST), np.float32)
    cw = np.zeros((CT, 2, ST, SPC // 2, 2, 2, 2, GC), np.float32)
    for r, (bn, cn) in enumerate((("ssm_b_re", "ssm_c_re"), ("ssm_b_im", "ssm_c_im"))):
        bv = f(bn)[0].reshape(2, CT, SPC // 2, 2, ST, GC)
        cv = f(cn)[0].reshape(2, CT, SPC // 2, 2, GC, ST)
        for g in range(2):
            bw[:, :, g, :, :, r, g, :] = bv[:, :, :, g].transpose(1, 2, 4, 0, 3)
            cw[:, g, :, :, :, r, g, :] = cv[:, :, :, g].transpose(1, 4, 2, 0, 3)
    return {
        "W": W, "keys": keys, "par": par, "bw": bw.reshape(CT, P, 4 * P), "cw": cw.reshape(CT, P, SPC * 64),
        "meta": f("meta_tokens"), "x": f("x")[0], "gffn": np.broadcast_to(f("norm_ffn")[0], (P, D)),
        "gfin": np.broadcast_to(f("norm_final"), (P, D)), "u_tab": f("peer_u")[0], "v_tab": f("peer_v")[0],
    }


ORDER = ["W", "keys", "par", "bw", "cw", "meta", "x", "gffn", "gfin", "u_tab", "v_tab"]


def kernel(**inputs):
    import concourse.bacc as bacc
    from concourse.bass_utils import run_bass_kernel_spmd

    nc = bacc.Bacc("TRN2", target_bir_lowering=False, num_devices=1)
    laid = lay_out(inputs)
    arrays = {n: np.ascontiguousarray(laid[n]) for n in ORDER}
    aps = [nc.dram_tensor(n, arrays[n].shape, F32, kind="ExternalInput").ap() for n in ORDER]
    out = nc.dram_tensor("out", (SEQ, D), F32, kind="ExternalOutput").ap()
    build(nc, *aps, out)
    r = run_bass_kernel_spmd(nc, [arrays], core_ids=[0])
    return r.results[0]["out"].reshape(1, SEQ, D)
```
